# Optimizing a Trainium2 kernel written in Bass

```python
import jax, jax.numpy as jnp
from jax import lax
import numpy as np

D_MODEL = 1024
BATCH = 1
SEQ = 256
DEPTH = 2

CTX_LEN = 256
GRID_W = 64
HEAD_DIM = 64
BRANCH_WIDTH = 512
N_BRANCH = 3
CONV_WIDTH = BRANCH_WIDTH
CONV_K = 3
NA_HEADS = BRANCH_WIDTH // HEAD_DIM
NA_WIDTH = NA_HEADS * HEAD_DIM
NA_ROWS_MAX = 8
NA_COLS = 16
NA_QCOL_BLOCK = 16
NA_KCOL_BLOCK = 32
SW_Q_HEADS = BRANCH_WIDTH // HEAD_DIM
SW_KV_HEADS = 2
SW_Q_WIDTH = SW_Q_HEADS * HEAD_DIM
SW_KV_WIDTH = SW_KV_HEADS * HEAD_DIM
SW_WINDOW = 128
SW_BLOCK = 128
ROPE_BASE = 10000.0
ROPE_AXIS_FREQS = HEAD_DIM // 4
N_EXPERTS = 16
EXPERT_FF = 1024
CAPACITY_FACTOR = 2
RMS_EPS = 1e-6
NEG = -1e30
IN_SPLITS = [CONV_WIDTH] * 3 + [NA_WIDTH] * 3 + [SW_Q_WIDTH, SW_KV_WIDTH, SW_KV_WIDTH] + [D_MODEL] * N_BRANCH
IN_WIDTH = 3 * CONV_WIDTH + 3 * NA_WIDTH + SW_Q_WIDTH + 2 * SW_KV_WIDTH + N_BRANCH * D_MODEL

kernel_name = 'hybrid_dit_conv_natten_swa_ec_moe'

def rms_norm(x, g):
    xf = x.astype(jnp.float32)
    y = xf * lax.rsqrt(jnp.mean(xf * xf, axis=-1, keepdims=True) + RMS_EPS)
    return (y * g.astype(jnp.float32)).astype(x.dtype)

def modulate(h, shift, scale):
    return h * (1 + scale) + shift

def split_in(z):
    offs, acc = [], 0
    for s in IN_SPLITS[:-1]:
        acc += s
        offs.append(acc)
    return jnp.split(z, offs, axis=-1)

def heads(t, n):
    return t.reshape(t.shape[0], t.shape[1], n, HEAD_DIM)

def axial_rope(n_tokens):
    t = jnp.arange(n_tokens, dtype=jnp.int32)
    row = (t // GRID_W).astype(jnp.float32)
    col = (t % GRID_W).astype(jnp.float32)
    inv = ROPE_BASE ** (-jnp.arange(ROPE_AXIS_FREQS, dtype=jnp.float32) / ROPE_AXIS_FREQS)
    ang = jnp.concatenate([row[:, None] * inv, col[:, None] * inv], axis=-1)
    return jnp.cos(ang), jnp.sin(ang)

def apply_rope(x, cos, sin):
    xf = x.astype(jnp.float32)
    half = HEAD_DIM // 2
    x1, x2 = xf[..., :half], xf[..., half:]
    cs, sn = cos[None, :, None, :], sin[None, :, None, :]
    return jnp.concatenate([x1 * cs - x2 * sn, x1 * sn + x2 * cs], axis=-1).astype(x.dtype)

def short_conv(u, w):
    return lax.conv_general_dilated(u, w[:, None, :], window_strides=(1,),
                                    padding=((CONV_K // 2, CONV_K // 2),),
                                    dimension_numbers=('NWC', 'WIO', 'NWC'),
                                    feature_group_count=u.shape[-1])

def context_attention(q, k, v, sink):
    B, L, H, Dh = q.shape
    Hk = k.shape[2]
    G = H // Hk
    qg = q.reshape(B, L, Hk, G, Dh)
    s = jnp.einsum('bqkgd,blkd->bkgql', qg, k).astype(jnp.float32) * (Dh ** -0.5)
    if sink is not None:
        sk = jnp.broadcast_to(sink.astype(jnp.float32).reshape(Hk, G, 1, 1), (B, Hk, G, L, 1))
        s = jnp.concatenate([s, sk], axis=-1)
    p = jax.nn.softmax(s, axis=-1)[..., :L].astype(v.dtype)
    o = jnp.einsum('bkgql,blkd->bqkgd', p, v)
    return o.reshape(B, L, H * Dh)

def neighbourhood_attention(q, k, v, kc, vc, rpb):
    B, S, H, Dh = q.shape
    rows = S // GRID_W
    kr = min(NA_ROWS_MAX, rows)
    ncb = GRID_W // NA_QCOL_BLOCK
    scale = Dh ** -0.5
    qcols = np.arange(GRID_W).reshape(ncb, NA_QCOL_BLOCK)
    kstart = np.clip(np.arange(ncb) * NA_QCOL_BLOCK - NA_COLS // 2, 0, GRID_W - NA_KCOL_BLOCK)
    kcols = kstart[:, None] + np.arange(NA_KCOL_BLOCK)
    cstart = np.clip(qcols - NA_COLS // 2, 0, GRID_W - NA_COLS)
    col_ok = (kcols[:, None, :] >= cstart[..., None]) & (kcols[:, None, :] < cstart[..., None] + NA_COLS)
    dcol_idx = np.clip(kcols[:, None, :] - qcols[..., None] + NA_COLS - 1, 0, 2 * NA_COLS - 2)
    qg = q.reshape(B, rows, ncb, NA_QCOL_BLOCK, H, Dh)
    kg = k.reshape(B, rows, GRID_W, H, Dh)
    vg = v.reshape(B, rows, GRID_W, H, Dh)
    n_loc = kr * NA_KCOL_BLOCK

    def row_block(r):
        rs = jnp.clip(r - kr // 2, 0, rows - kr)
        kb = lax.dynamic_slice_in_dim(kg, rs, kr, axis=1)[:, :, kcols]
        vb = lax.dynamic_slice_in_dim(vg, rs, kr, axis=1)[:, :, kcols]
        qb = lax.dynamic_index_in_dim(qg, r, axis=1, keepdims=False)
        s_loc = jnp.einsum('bjqhd,brjkhd->bhjqrk', qb, kb).astype(jnp.float32) * scale
        dr_idx = rs + jnp.arange(kr) - r + NA_ROWS_MAX - 1
        bias = rpb[:, dr_idx[:, None, None, None], dcol_idx[None]]
        bias = bias.transpose(0, 2, 3, 1, 4).astype(jnp.float32)
        s_loc = jnp.where(col_ok[:, :, None, :], s_loc + bias[None], NEG)
        s_loc = s_loc.reshape(B, H, ncb, NA_QCOL_BLOCK, n_loc)
        s_ctx = jnp.einsum('bjqhd,blhd->bhjql', qb, kc).astype(jnp.float32) * scale
        p = jax.nn.softmax(jnp.concatenate([s_loc, s_ctx], axis=-1), axis=-1).astype(v.dtype)
        p_loc = p[..., :n_loc].reshape(B, H, ncb, NA_QCOL_BLOCK, kr, NA_KCOL_BLOCK)
        return (jnp.einsum('bhjqrk,brjkhd->bjqhd', p_loc, vb)
                + jnp.einsum('bhjql,blhd->bjqhd', p[..., n_loc:], vc))

    out = lax.map(row_block, jnp.arange(rows))
    return jnp.moveaxis(out, 0, 1).reshape(B, S, H * Dh)

def window_attention(q, k, v, kc, vc, sink):
    B, S, H, Dh = q.shape
    Hk = k.shape[2]
    G = H // Hk
    L = kc.shape[1]
    nb = S // SW_BLOCK
    span = SW_BLOCK + 2 * SW_WINDOW
    scale = Dh ** -0.5
    pad = ((0, 0), (SW_WINDOW, SW_WINDOW), (0, 0), (0, 0))
    kpad, vpad = jnp.pad(k, pad), jnp.pad(v, pad)
    qall = q.reshape(B, nb, SW_BLOCK, Hk, G, Dh)
    sk = jnp.broadcast_to(sink.astype(jnp.float32).reshape(Hk, G, 1, 1), (B, Hk, G, SW_BLOCK, 1))

    def block(n):
        start = n * SW_BLOCK
        kb = lax.dynamic_slice_in_dim(kpad, start, span, axis=1)
        vb = lax.dynamic_slice_in_dim(vpad, start, span, axis=1)
        qb = lax.dynamic_index_in_dim(qall, n, axis=1, keepdims=False)
        qpos = start + jnp.arange(SW_BLOCK)
        kpos = start - SW_WINDOW + jnp.arange(span)
        ok = (jnp.abs(qpos[:, None] - kpos[None, :]) <= SW_WINDOW) & (kpos[None, :] >= 0) & (kpos[None, :] < S)
        s_loc = jnp.einsum('bqkgd,blkd->bkgql', qb, kb).astype(jnp.float32) * scale
        s_loc = jnp.where(ok, s_loc, NEG)
        s_ctx = jnp.einsum('bqkgd,blkd->bkgql', qb, kc).astype(jnp.float32) * scale
        p = jax.nn.softmax(jnp.concatenate([s_loc, s_ctx, sk], axis=-1), axis=-1).astype(v.dtype)
        return (jnp.einsum('bkgql,blkd->bqkgd', p[..., :span], vb)
                + jnp.einsum('bkgql,blkd->bqkgd', p[..., span:span + L], vc))

    out = lax.map(block, jnp.arange(nb))
    return jnp.moveaxis(out, 0, 1).reshape(B, S, H * Dh)

def merge_branches(outs, gate_logits, w_branch, w_out):
    merged = jax.nn.sigmoid(gate_logits[0]) * (outs[0] @ w_branch[0])
    for i in range(1, N_BRANCH):
        merged = merged + jax.nn.sigmoid(gate_logits[i]) * (outs[i] @ w_branch[i])
    return merged @ w_out

def expert_choice_ffn(h, w_router, w_gate, w_up, w_down):
    B, N, D = h.shape
    cap = CAPACITY_FACTOR * N // N_EXPERTS
    aff = jax.nn.softmax((h @ w_router).astype(jnp.float32), axis=-1)
    gate, idx = lax.top_k(jnp.swapaxes(aff, 1, 2), cap)
    bidx = jnp.arange(B)[:, None, None]
    xe = h[bidx, idx]
    a = jnp.einsum('becd,edf->becf', xe, w_gate)
    u = jnp.einsum('becd,edf->becf', xe, w_up)
    ye = jnp.einsum('becf,efd->becd', jax.nn.silu(a) * u, w_down) * gate[..., None].astype(h.dtype)
    return jnp.zeros_like(h).at[bidx, idx].add(ye)

def setup_inputs(seed: int = 0) -> dict:
    key = jax.random.key(seed)
    ks = jax.random.split(key, 19)
    D = D_MODEL

    def nrm(k, shape, scale):
        return jax.random.normal(k, shape, jnp.float32) * scale

    return {
        'x': nrm(ks[0], (BATCH, SEQ, D), 1.0),
        'c': nrm(ks[1], (BATCH, D), 1.0),
        'ctx': nrm(ks[2], (BATCH, CTX_LEN, D), 1.0),
        'c_ctx': nrm(ks[3], (D,), 1.0),
        'w_ada': nrm(ks[4], (DEPTH, D, 6 * D), 0.5 * D ** -0.5),
        'b_ada': nrm(ks[5], (DEPTH, 6 * D), 0.02),
        'g_mix': 1.0 + nrm(ks[6], (DEPTH, D), 0.02),
        'w_in': nrm(ks[7], (DEPTH, D, IN_WIDTH), D ** -0.5),
        'conv_w': nrm(ks[8], (DEPTH, CONV_K, CONV_WIDTH), CONV_K ** -0.5),
        'na_rpb': nrm(ks[9], (DEPTH, NA_HEADS, 2 * NA_ROWS_MAX - 1, 2 * NA_COLS - 1), 0.1),
        'sw_sink': nrm(ks[10], (DEPTH, SW_Q_HEADS), 0.5),
        'w_branch': nrm(ks[11], (DEPTH, N_BRANCH, BRANCH_WIDTH, D), BRANCH_WIDTH ** -0.5),
        'w_out': nrm(ks[12], (DEPTH, D, D), D ** -0.5),
        'g_ffn': 1.0 + nrm(ks[13], (DEPTH, D), 0.02),
        'w_router': nrm(ks[14], (DEPTH, D, N_EXPERTS), D ** -0.5),
        'w_exp_gate': nrm(ks[15], (DEPTH, N_EXPERTS, D, EXPERT_FF), D ** -0.5),
        'w_exp_up': nrm(ks[16], (DEPTH, N_EXPERTS, D, EXPERT_FF), D ** -0.5),
        'w_exp_down': nrm(ks[17], (DEPTH, N_EXPERTS, EXPERT_FF, D), EXPERT_FF ** -0.5),
        'g_final': 1.0 + nrm(ks[18], (D,), 0.02),
    }

def reference(x, c, ctx, c_ctx, w_ada, b_ada, g_mix, w_in, conv_w, na_rpb, sw_sink, w_branch, w_out,
              g_ffn, w_router, w_exp_gate, w_exp_up, w_exp_down, g_final):
    S = x.shape[1]
    cos, sin = axial_rope(S)
    xc = ctx
    for l in range(DEPTH):
        last = l == DEPTH - 1
        mod = (jax.nn.silu(c) @ w_ada[l] + b_ada[l])[:, None, :]
        mod_c = (jax.nn.silu(c_ctx)[None] @ w_ada[l] + b_ada[l])[:, None, :]
        sh1, sc1, gt1, sh2, sc2, gt2 = jnp.split(mod, 6, axis=-1)
        csh1, csc1, cgt1, csh2, csc2, cgt2 = jnp.split(mod_c, 6, axis=-1)

        h = modulate(rms_norm(x, g_mix[l]), sh1, sc1)
        hc = modulate(rms_norm(xc, g_mix[l]), csh1, csc1)
        a_b, a_c, a_x, na_q, na_k, na_v, sw_q, sw_k, sw_v, ga, gb, gc = split_in(h @ w_in[l])
        ca_b, ca_c, ca_x, cna_q, cna_k, cna_v, csw_q, csw_k, csw_v, cga, cgb, cgc = split_in(hc @ w_in[l])
        kc_na, vc_na = heads(cna_k, NA_HEADS), heads(cna_v, NA_HEADS)
        kc_sw, vc_sw = heads(csw_k, SW_KV_HEADS), heads(csw_v, SW_KV_HEADS)

        o_a = a_b * short_conv(a_c * a_x, conv_w[l])
        o_b = neighbourhood_attention(heads(na_q, NA_HEADS), heads(na_k, NA_HEADS), heads(na_v, NA_HEADS),
                                      kc_na, vc_na, na_rpb[l])
        o_c = window_attention(apply_rope(heads(sw_q, SW_Q_HEADS), cos, sin),
                               apply_rope(heads(sw_k, SW_KV_HEADS), cos, sin),
                               heads(sw_v, SW_KV_HEADS), kc_sw, vc_sw, sw_sink[l])
        x = x + gt1 * merge_branches((o_a, o_b, o_c), (ga, gb, gc), w_branch[l], w_out[l])
        if not last:
            co_a = ca_b * short_conv(ca_c * ca_x, conv_w[l])
            co_b = context_attention(heads(cna_q, NA_HEADS), kc_na, vc_na, None)
            co_c = context_attention(heads(csw_q, SW_Q_HEADS), kc_sw, vc_sw, sw_sink[l])
            xc = xc + cgt1 * merge_branches((co_a, co_b, co_c), (cga, cgb, cgc), w_branch[l], w_out[l])

        x = x + gt2 * expert_choice_ffn(modulate(rms_norm(x, g_ffn[l]), sh2, sc2),
                                        w_router[l], w_exp_gate[l], w_exp_up[l], w_exp_down[l])
        if not last:
            xc = xc + cgt2 * expert_choice_ffn(modulate(rms_norm(xc, g_ffn[l]), csh2, csc2),
                                               w_router[l], w_exp_gate[l], w_exp_up[l], w_exp_down[l])
    return rms_norm(x, g_final)


_drawn_inputs = setup_inputs


def setup_inputs(seed=0):
    import zlib

    import numpy as np

    out = dict(_drawn_inputs(seed))
    spreads = {}
    factors = {'g_mix': 4.159, 'na_rpb': 45.019, 'sw_sink': 8.0, 'g_ffn': 5.275, 'g_final': 8.302}
    for name, (base, spread) in spreads.items():
        noise = np.random.default_rng([zlib.crc32(name.encode()), seed]).standard_normal(out[name].shape)
        drawn = base * np.exp(spread * noise) if base else spread * noise
        out[name] = __import__('jax').numpy.asarray(drawn.astype(out[name].dtype))
    for name, factor in factors.items():
        out[name] = (out[name] * factor).astype(out[name].dtype)
    return out
```

```python
from contextlib import ExitStack

import numpy as np

import concourse.bass as bass
from concourse import mybir

D = 1024
SEQ = 256
CTX = 256
TOK = SEQ + CTX
DEPTH = 2
GRID_W = 64
HD = 64
BW = 512
NE = 16
FF = 1024
CAP = 2 * SEQ // NE
KD = D // 128
KB = BW // 128
NTT = TOK // 128
RPB_R, RPB_C = 15, 31
RPB_REP = 65
NEG = -1e30
EPS = 1e-6
SLOT = 4096
NSLOT = 6
SLAB = 56280
NBLK = 3
COL = dict(ab=0, ac=512, ax=1024, nq=1536, nk=2048, nv=2560, sq=3072, sk=3584, sv=3712, gate=3840)
SH1, SC1, GT1, SH2, SC2, GT2V = range(6)


def shape_constants():
    p = np.arange(128)
    ident = np.eye(128, dtype=np.float32)
    t = np.arange(SEQ)
    inv = (np.float32(10000.0) ** (-np.arange(16, dtype=np.float32) / np.float32(16))).astype(np.float32)
    ang = np.concatenate([(t // GRID_W).astype(np.float32)[:, None] * inv,
                          (t % GRID_W).astype(np.float32)[:, None] * inv], axis=1)
    rope = np.stack([np.cos(ang).T[p % 32], np.sin(ang).T[p % 32]], axis=1).astype(np.float32)
    rot = np.zeros((128, 128), np.float32)
    for o in range(128):
        if o % 64 < 32:
            rot[o + 32, o] = -1.0
        else:
            rot[o - 32, o] = 1.0
    q = p[:, None, None] + 128 * np.arange(2)[None, :, None]
    swmask = np.where(np.abs(q - t[None, None, :]) <= 128, 0.0, NEG).astype(np.float32)
    c = p[:, None] % GRID_W
    kc = t[None, :] % GRID_W
    start = np.clip(c - 8, 0, GRID_W - 16)
    namask = np.where((kc >= start) & (kc < start + 16), 0.0, NEG).astype(np.float32)
    sel = np.zeros((128, 2, 128), np.float32)
    for s in range(2):
        sel[s::32, s, :] = 1.0
    slots = np.tile(np.arange(1, CAP + 1, dtype=np.float32), (128, 1))
    flat = [ident, rope.reshape(128, -1), rot, swmask.reshape(128, -1), namask, sel.reshape(128, -1), slots]
    return np.ascontiguousarray(np.concatenate(flat, axis=1))


CONST_W = [128, 512, 128, 512, 256, 256, CAP]


class Step:

    def __init__(self, ac_tile=None, act=None, arrive=None, arrived=None, at=None, b=None, bank=None, before=None, bias=None,
                 bias_before=None, blk=None, br=None, c_tile=None, chunk=None, code=None, col=None, d=None, d_tile=None,
                 dve=None, end=None, expert=None, first=None, gate=None, grp=None, gt_free=None, half=None, hh=None, hts=None,
                 i=None, info=None, k=None, kind=None, kk=None, l=None, layer=None, lg=None, lt=None, mods=None, n=None,
                 nk=None, ns=None, ntt=None, o_ready=None, o_ready_need=None, ord=None, out=None, out_tile=None, p=None,
                 parts=None, pt_before=None, qt=None, ready=None, recent=None, ref=None, rope=None, rot_tile=None, s=None,
                 set=None, sets=None, slot=None, split_end=None, src=None, sum=None, tile=None, tiles=None, u=None, unit=None,
                 units=None, used_tile=None, v=None, v_ready=None, which=None, width=None, x_updated=None):
        self.ac_tile = ac_tile
        self.act = act
        self.arrive = arrive
        self.arrived = arrived
        self.at = at
        self.b = b
        self.bank = bank
        self.before = before
        self.bias = bias
        self.bias_before = bias_before
        self.blk = blk
        self.br = br
        self.c_tile = c_tile
        self.chunk = chunk
        self.code = code
        self.col = col
        self.d = d
        self.d_tile = d_tile
        self.dve = dve
        self.end = end
        self.expert = expert
        self.first = first
        self.gate = gate
        self.grp = grp
        self.gt_free = gt_free
        self.half = half
        self.hh = hh
        self.hts = hts
        self.i = i
        self.info = info
        self.k = k
        self.kind = kind
        self.kk = kk
        self.l = l
        self.layer = layer
        self.lg = lg
        self.lt = lt
        self.mods = mods
        self.n = n
        self.nk = nk
        self.ns = ns
        self.ntt = ntt
        self.o_ready = o_ready
        self.o_ready_need = o_ready_need
        self.ord = ord
        self.out = out
        self.out_tile = out_tile
        self.p = p
        self.parts = parts
        self.pt_before = pt_before
        self.qt = qt
        self.ready = ready
        self.recent = recent
        self.ref = ref
        self.rope = rope
        self.rot_tile = rot_tile
        self.s = s
        self.set = set
        self.sets = sets
        self.slot = slot
        self.split_end = split_end
        self.src = src
        self.sum = sum
        self.tile = tile
        self.tiles = tiles
        self.u = u
        self.unit = unit
        self.units = units
        self.used_tile = used_tile
        self.v = v
        self.v_ready = v_ready
        self.which = which
        self.width = width
        self.x_updated = x_updated


class Plan:

    def __init__(self):
        self.steps = [[] for _ in range(DEPTH + 1)]
        self.layer = 0
        self.tiles = self.act = self.dve = 0
        self.recent = [None] * NBLK
        self.blocks = []
        self.loads = 0
        self.arrive = [0] * NSLOT
        self.occupant = [None] * NSLOT
        self.units = self.sets = self.biases = 0
        self.mods = 0
        self.bias_unit = [None, None]
        self.ropes = 0
        self.obs = 0
        self.sums = 0
        self.gt_free = None
        self.pt_before = [None, None]
        self.deferred = []
        self.scored = self.turned = None

    def add(self, kind, **kw):
        s = Step(kind=kind, layer=self.layer, **kw)
        self.steps[self.layer].append(s)
        return s

    def tile(self, act=False, dve=False):
        n = self.tiles
        self.tiles += 1
        t = Step(n=n, bank=n % NBLK, before=self.recent[n % NBLK], ready=n + 1, act=None, dve=None)
        if act:
            self.act += 1
            t.act = self.act
        if dve:
            self.dve += 1
            t.dve = self.dve
        self.recent[n % NBLK] = t
        return t

    def load(self, parts):
        slot = self.loads % 2
        self.loads += 1
        self.arrive[slot] += 16 * len(parts)
        c = Step(slot=slot, arrived=self.arrive[slot], before=self.occupant[slot], parts=parts, split_end=None, used_tile=None)
        self.occupant[slot] = c
        self.add("load", chunk=c)
        return c

    def block(self, chunk, at, width, col, kk, n, src, out, tile, **kw):
        b = Step(b=len(self.blocks), chunk=chunk, at=at, width=width, col=col, kk=kk, n=n, src=src, tile=tile, out=out, **kw)
        self.blocks.append(b)
        chunk.split_end = b.b + 1
        return b

    def flush(self):
        todo, self.deferred = self.deferred, []
        for f in todo:
            f()


def ksteps(P, b):
    return [("k", b, k) for k in range(b.kk)]


WAHEAD = 2
NWS = WAHEAD + 1


def make_plan():
    P = Plan()

    def finish_block(b):
        if not b.tile.dve:
            P.flush()
        P.add("done", blk=b)
        P.flush()
        if b.out in ("v", "out"):
            def turn_back():
                b.out_tile = P.tile(dve=True)
                P.add("finish", blk=b)
            P.deferred.append(turn_back)
        elif b.out in ("sk", "sq"):
            def rope():
                b.rot_tile = P.tile(dve=True)
                P.ropes += 1
                b.rope = P.ropes
                b.info.ready = ("qk_ready", P.ropes)
                P.add("finish", blk=b)
            P.deferred.append(rope)

    def emit(atom):
        kind = atom[0]
        if kind == "k":
            P.add("k", blk=atom[1], k=atom[2])
        elif kind == "done":
            finish_block(atom[1])
        elif kind == "call":
            atom[1]()
        else:
            raise ValueError(kind)

    def run(atoms):
        for a in atoms:
            emit(a)

    def ada(l, c):
        def go():
            ch = P.load([(0, (8, 512), ("w_ada", l, 512 * c, 512))])
            v, half = c // 2, c % 2
            mm = P.tile(dve=True)
            ch.used_tile = mm.ready
            s = P.add("ada", l=l, v=v, half=half, chunk=ch, tile=mm)

            def turn():
                if v == GT2V:
                    s.out = [P.tile(dve=True) for _ in range(2)]
                else:
                    s.out = [P.tile(dve=True)]
                    P.mods += 1
                P.add("ada2", l=l, v=v, half=half, out=s.out, tile=mm)
            P.deferred.append(turn)
        return go

    for l in range(DEPTH):
        P.layer = l
        last = l == DEPTH - 1
        NT = SEQ if last else TOK
        P.first_tile = P.tiles
        if l == 0:
            P.add("pre", tile=P.tile(act=True))
            for c in range(4):
                ada(0, c)()
                P.flush()
        P.add("norm", which=0, ntt=4)
        for k in range(KD):
            P.add("trmod", which=0, k=k, ntt=4, tile=P.tile(act=True), mods=P.mods, hts=8 * l + k)

        def col_chunk(name, l=l):
            return P.load([(0, (8, 512), ("w_in", l, COL[name], 512))])
        ac_tiles = []
        for name in ("ac", "ax", "ab"):
            ch = col_chunk(name)
            for i in range(KB):
                t = P.tile(act=name == "ac", dve=name != "ac")
                b = P.block(ch, 0, 512, 128 * i, 8, NT, "h", name, t, i=i)
                if name == "ac":
                    ac_tiles[i:] = [t]
                b.ac_tile = ac_tiles[i]
                if name == "ab":
                    P.obs += 1
                    b.o_ready = P.obs
                run(ksteps(P, b) + [("done", b)])
        o_conv = P.obs

        ch = col_chunk("nv")
        sv = None
        for i in range(KB + 1):
            if i == KB:
                ch = P.load([(0, (8, 128), ("w_in", l, COL["sv"], 128))])
            b = P.block(ch, 0, 512 if i < KB else 128, 128 * i if i < KB else 0, 8, TOK, "h", "v", P.tile(act=True), i=i)
            run(ksteps(P, b) + [("done", b)])
            sv = b

        def qk(br, p, l=l, NT=NT):
            info = Step(br=br, p=p)
            atoms = []
            if br == "na":
                ch = P.load([(0, (8, 128), ("w_in", l, COL["nq"] + 128 * p, 128)),
                             (1024, (8, 128), ("w_in", l, COL["nk"] + 128 * p, 128))])
                for j, (name, n) in enumerate((("nq", NT), ("nk", TOK))):
                    t = None
                    b = P.block(ch, 1024 * j, 128, 0, 8, n, "h", name, None, p=p, info=info)
                    atoms += [("call", (lambda b=b: open_tile(b, dict(act=True, dve=True))))] + ksteps(P, b)
                    def fin(b=b):
                        finish_block(b)
                        info.ready = ("dve_evicted", b.tile.dve)
                    atoms.append(("call", fin))
            else:
                names = (("sk", TOK),) if p == 0 else ()
                names += (("sq", NT),)
                parts = []
                for j, (name, n) in enumerate(names):
                    c = COL["sk"] if name == "sk" else COL["sq"] + 128 * p
                    parts.append((1024 * j, (8, 128), ("w_in", l, c, 128)))
                ch = P.load(parts)
                for j, (name, n) in enumerate(names):
                    b = P.block(ch, 1024 * j, 128, 0, 8, n, "h", name, None, p=p, info=info)
                    atoms += [("call", (lambda b=b: open_tile(b, dict(act=True))))] + ksteps(P, b)
                    atoms.append(("done", b))
            return info, atoms

        def open_tile(b, kw):
            b.tile = P.tile(**kw)

        def dpair(i, d2, l=l, NT=NT):
            ch = P.load([(0, (8, 256), ("w_in", l, COL["gate"] + D * i + 256 * d2, 256)),
                         (2048, (4, 256), ("w_branch", l * 3 + i, 256 * d2, 256))])
            atoms = []
            for j in range(2):
                d = 2 * d2 + j
                g = P.block(ch, 0, 256, 128 * j, 8, NT, "h", "gate", None, i=i, d=d)
                atoms += [("call", (lambda b=g: open_tile(b, dict(act=True))))] + ksteps(P, g)
                r = P.block(ch, 2048, 256, 128 * j, 4, NT, "o%d" % i, "br", None, i=i, d=d, gate=g)
                def fin_g(b=g):
                    b.gt_free = P.gt_free
                    finish_block(b)
                atoms.append(("call", fin_g))
                atoms += [("call", (lambda b=r: open_tile(b, dict(dve=True))))] + ksteps(P, r)
                def fin_r(b=r):
                    if i == 0:
                        P.gt_free = ("dve_evicted", b.tile.dve)
                    else:
                        P.sums += 1
                        P.gt_free = ("mrg_ready", P.sums)
                    b.sum = P.sums
                    finish_block(b)
                atoms.append(("call", fin_r))
            return atoms

        def attention(br, p, info, fill):
            units = []
            for grp in range(1 if last else 2):
                st = Step(br=br, p=p, grp=grp, set=P.sets, first=P.units + len(units), v_ready=sv.out_tile.dve)
                P.sets += 1
                P.obs += 1
                st.o_ready = P.obs
                st.pt_before = P.pt_before[grp]
                P.pt_before[grp] = P.sets
                for hh in range(2):
                    for j in range(2):
                        units.append(Step(br=br, p=p, hh=hh, qt=2 * grp + j, u=P.units + len(units), info=info,
                                          nk=TOK if grp == 0 else CTX, set=st, end=hh == 1 and j == 1, bias=None, layer=l))
                st.end = P.units + len(units)
            P.units += len(units)
            for x in units:
                if br == "na" and x.qt < 2:
                    P.biases += 1
                    x.bias = P.biases
                    x.bias_before = P.bias_unit[x.bias % 2]
                    P.bias_unit[x.bias % 2] = x.u + 1
                    P.add("bias", unit=x)
            nk_atoms = sum(a[0] == "k" for a in fill)
            per = -(-nk_atoms // len(units)) if nk_atoms else 0
            fill = list(fill)

            def piece():
                n = 0
                while fill and n < per:
                    a = fill.pop(0)
                    emit(a)
                    n += a[0] == "k"
                while fill and fill[0][0] != "k":
                    emit(fill.pop(0))

            for i, x in enumerate(units):
                normalise()
                P.add("score", unit=x)
                piece()
                turn()
                P.scored = x
            run(fill)

        def normalise():
            if P.scored:
                P.add("normalise", unit=P.scored)

        def turn():
            if P.turned:
                P.add("pv", set=P.turned.set)
                P.turned = None
            if P.scored:
                P.add("turn", unit=P.scored)
                if P.scored.end:
                    P.turned = P.scored
                P.scored = None

        P.o_need = {0: o_conv}
        info, atoms = qk("na", 0)
        run(atoms)
        for p in range(KB):
            if p + 1 < KB:
                nxt, atoms = qk("na", p + 1)
            else:
                nxt, atoms = qk("sw", 0)
            attention("na", p, info, atoms + dpair(0, p))
            info = nxt
        o_na = P.obs
        for p in range(KB):
            nxt, atoms = qk("sw", p + 1) if p + 1 < KB else (None, [])
            attention("sw", p, info, atoms + dpair(1, p))
            info = nxt
        o_sw = P.obs
        normalise()
        turn()
        turn()
        extra = [ada(l, c) for c in (4, 5, 10, 11, 6, 7, 8, 9)]
        if not last:
            extra += [ada(l + 1, c) for c in range(4)]
        for d2 in range(4):
            atoms = dpair(2, d2)
            mid = len(atoms) // 2
            run(atoms[:mid])
            if d2 == 0:
                P.add("gt2_bias", l=l, sets=P.sets)
            extra.pop(0)()
            run(atoms[mid:])
            extra.pop(0)()
        P.c_tile = P.tiles
        stage_c_end = P.tiles
        for b in [x for x in P.blocks if x.src[0] == "o" and x.o_ready_need is None]:
            b.o_ready_need = {"o0": o_conv, "o1": o_na, "o2": o_sw}[b.src]
        for half in range(2):
            ch = P.load([(0, (8, 512), ("w_out", l, 512 * half, 512))])
            for i in range(4):
                b = P.block(ch, 0, 512, 128 * i, 8, NT, "m", "out", P.tile(act=True), d=4 * half + i, ord=8 * l + 4 * half + i)
                run(ksteps(P, b))
                b.mods = P.mods
                run([("done", b)])
                if extra and i % 2:
                    extra.pop(0)()
        P.flush()
        dense_end = P.tiles
        x_updated = b.out_tile.dve

        ns = 1 if last else 2
        P.add("norm", which=1, ntt=2 * ns, x_updated=x_updated)
        for k in range(KD):
            P.add("trmod", which=1, k=k, ntt=2 * ns, tile=P.tile(act=True), mods=P.mods, hts=None)
        P.add("route", ns=ns, lg=P.tile(act=True), lt=P.tile(dve=True), at=P.tile(dve=True), code=P.tile(dve=True))
        for s in range(ns):
            for k in range(KD):
                P.add("gather", ns=ns, s=s, k=k, tile=P.tile(act=k % 2 == 0, dve=k % 2 == 1))
        P.add("gates", ns=ns, tiles=[[P.tile(act=gp == 0, dve=gp == 1) for gp in range(2)] for s in range(ns)])
        m = P.add("moe", ns=ns, arrive=list(P.arrive), before=list(P.occupant), tiles=P.tiles,
                  c_tile=stage_c_end, d_tile=dense_end, recent=list(P.recent), act=P.act, dve=P.dve)
        for j in range(NSLOT):
            P.arrive[j] += 16 * NE
            P.occupant[j] = Step(expert=l, slot=j)
        P.recent = [None] * NBLK
        if P.loads % 2:
            P.loads += 1
    P.layer = DEPTH
    P.final_before = P.occupant[0]
    P.add("final")

    for l in range(DEPTH):
        out, layer_blocks = [], [s.blk for s in P.steps[l] if s.kind == "k" and s.k == 0]
        ahead = {a.b: c for a, c in zip(layer_blocks, layer_blocks[WAHEAD:])}
        for s in P.steps[l]:
            if s.kind == "k" and s.k == 0 and s.blk.b in ahead:
                out.append(Step(kind="split", layer=l, blk=ahead[s.blk.b]))
            out.append(s)
            if s.kind == "norm" and s.which == 0:
                out += [Step(kind="split", layer=l, blk=b) for b in layer_blocks[:WAHEAD]]
        P.steps[l] = out
    return P


def hybrid_dit_kernel(nc, A, out):
    f32 = mybir.dt.float32
    f32r = mybir.dt.float32r
    ALU = mybir.AluOpType
    ACT = mybir.ActivationFunctionType
    AX = mybir.AxisListType
    P = make_plan()
    ctx = ExitStack()
    with ctx:
        slab = ctx.enter_context(nc.sbuf_tensor("slab", [128, SLAB], f32))
        del slab
        base = nc.sbuf_base - SLAB * 4
        cursor = [base]

        def region(nbytes):
            at = cursor[0]
            cursor[0] += nbytes
            assert cursor[0] <= base + SLAB * 4, cursor[0] - base
            return at

        def sb(name, shape, at, dt=f32):
            return nc.alloc_sbuf_tensor_at(name, shape, dt, offset=at)

        R_X = region(16384)
        R_RING = region(NSLOT * 16384)
        R_HT = region(32768)
        R_WS = region(8192 * NWS)
        R_MRG = region(16384)
        R_PT = region(12288)
        R_P = region(4096)
        R_BIAS = region(2048)
        R_GT = region(2048)
        R_QT = region(2048)
        R_VSW = region(2048)

        X = sb("X", [128, NTT, D], R_X)
        ring = [sb(f"ring{j}", [128, SLOT], R_RING + 16384 * j) for j in range(NSLOT)]
        R_O = R_RING + 2 * 16384
        R_Q = R_RING + 4 * 16384
        OH = [sb(f"OH{i}", [128, KB, TOK], R_O + 16384 * i, f32r) for i in range(2)]
        OL = [sb(f"OL{i}", [128, KB, TOK], R_O + 16384 * i + 8192, f32r) for i in range(2)]
        V = sb("V", [128, NTT, BW], R_Q)
        VS = sb("VS", [128, NTT, 128], R_VSW)
        dup = [sb(f"dup{i}", [128, 2, 2, TOK], R_Q + 8192 + 8192 * i, f32r) for i in range(2)]
        stk = [sb(f"stk{i}", [128, 2, TOK], R_Q + 24576 + 4096 * i, f32r) for i in range(2)]
        AC = sb("AC", [128, KB, TOK], R_Q + 8192)
        U = sb("U", [128, KB, 2, SEQ + 2], R_Q + 16384)
        MH = sb("MH", [128, KD, TOK], R_Q, f32r)
        ML = sb("ML", [128, KD, TOK], R_Q + 16384, f32r)
        RPBT = [sb(f"RPBT{l}", [8 * RPB_R, RPB_REP, RPB_C], R_O + 16384 + 8192 * l) for l in range(DEPTH)]
        tiled = [nc.dram_tensor(f"rpb_tiled{l}", (8 * RPB_R, RPB_REP * RPB_C), f32, kind="Internal").ap() for l in range(DEPTH)]
        HH = sb("HH", [128, KD, TOK], R_HT, f32r)
        HL = sb("HL", [128, KD, TOK], R_HT + 16384, f32r)
        WH = [sb(f"WH{i}", [128, KD, 128], R_WS + 8192 * i, f32r) for i in range(NWS)]
        WL = [sb(f"WL{i}", [128, KD, 128], R_WS + 8192 * i + 4096, f32r) for i in range(NWS)]
        MRG = sb("MRG", [128, KD, TOK], R_MRG)
        PTL = sb("PTL", [128, 2, 4, SEQ], R_PT)
        PTC = sb("PTC", [128, 2, 2, SEQ], R_PT + 8192)
        PB = [sb(f"PB{i}", [128, TOK], R_P + 2048 * i) for i in range(2)]
        FT = [sb(f"FT{i}", [128, TOK], R_P + 2048 * i) for i in range(2)]
        YT = [sb(f"YT{i}", [128, TOK], R_P + 2048 * i) for i in range(2)]
        CT = sb("CT", [128, 2, SEQ], R_P)
        BIAS = [sb(f"BIAS{i}", [128, SEQ], R_BIAS + 1024 * i) for i in range(2)]
        GT = sb("GT", [128, TOK], R_GT)
        QT = sb("QT", [128, TOK], R_QT)
        VT = [sb(f"VT{i}", [128, TOK], at_) for i, at_ in enumerate((R_GT, R_QT))]
        MB = sb("MB", [128, TOK], R_PT + 8192)
        XN = sb("XN", [128, NTT, D], R_MRG)
        H2 = sb("H2", [128, KD, TOK], R_HT)
        LG = sb("LG", [NE, TOK], R_HT + 16384)
        WK = sb("WK", [32, SEQ], R_HT + 18432)
        MASK = sb("MASK", [32, SEQ], R_HT + 19456)
        CUM = sb("CUM", [32, SEQ], R_HT + 20480)
        CODE = sb("CODE", [32, SEQ], R_HT + 21504)
        CODT = sb("CODT", [128, 2, 2, NE], R_HT + 22528)
        XE = [sb(f"XE{n}", [128, KD, NE, n * CAP], R_HT) for n in (1, 2)]
        SELT = sb("SELT", [128, 2, 2, NE, CAP], R_WS)
        ST = sb("ST", [128, 4, 2, SEQ], R_WS + 8192)
        GT2 = sb("GT2", [128, 2, D], R_PT)
        TH = sb("TH", [128, 512], R_PT + 8192)
        HID = sb("HID", [128, 512], R_PT + 10240)
        XEB = [sb(f"XEB{i}", [128, KD, 64], R_P + 2048 * i) for i in range(2)]
        HIDT = sb("HIDT", [128, KD, 64], R_BIAS)
        STB = sb("STB", [128, 2, SEQ], R_GT)
        YE = sb("YE", [128, 2, D], R_MRG)
        TMP = sb("TMP", [128, 512], R_MRG + 8192)
        GF = sb("GF", [128, D], R_RING)
        CONST = sb("CONST", [128, sum(CONST_W)], region(4 * sum(CONST_W)))
        at = [sum(CONST_W[:i]) for i in range(len(CONST_W) + 1)]
        IDENT = CONST[:, at[0]:at[1]]
        ROPE = CONST[:, at[1]:at[2]].rearrange("p (a t) -> p a t", a=2)
        ROT = CONST[:, at[2]:at[3]]
        SWM = CONST[:, at[3]:at[4]].rearrange("p (a t) -> p a t", a=2)
        NAM = CONST[:, at[4]:at[5]]
        SELB = CONST[:, at[5]:at[6]].rearrange("p (a t) -> p a t", a=2)
        SLOTS = CONST[:, at[6]:at[7]]
        NROW2 = 16 + DEPTH * 12
        COLS = sb("COLS", [128, 128 + NROW2], region(4 * (128 + NROW2)))
        ROWS = sb("ROWS", [128, 2, 128], R_P)
        RPB = sb("RPB", [8 * RPB_R, DEPTH, RPB_C], R_QT)
        CS = sb("CS", [128, KD, 32], region(1024))
        MOD = sb("MOD", [128, DEPTH, 6, KD, 2], region(4 * DEPTH * 96))
        WR = sb("WR", [128, DEPTH, KD, NE], region(4 * DEPTH * 128))
        SINK = sb("SINK", [128, DEPTH, 8], region(4 * DEPTH * 8))
        AFF = sb("AFF", [128, 2, 2, NE], region(256))
        SM = sb("SM", [128, 112], region(448))
        SS, VV, SD, RS, NW = (SM[:, 4 * i:4 * i + 4] for i in range(5))
        RMX, RSUM = SM[:, 20:24], SM[:, 24:28]
        M8 = SM[0:32, 28:36]
        MX = [SM[:, 36 + 2 * i:38 + 2 * i] for i in range(2)]
        NM = [SM[:, 40 + i:41 + i] for i in range(2)]
        ES = [SM[:, 44 + 3 * i:47 + 3 * i] for i in range(2)]
        RSM = [SM[:, 50 + i:51 + i] for i in range(2)]
        RED = SM[:, 52:60].rearrange("p (k s) -> p k s", k=4)
        TC = SM[:, 60:76]
        T2 = SM[:, 76:92]
        PRIME = SM[:, 92:112]
        BANK = [ctx.enter_context(nc.psum_tensor(f"bank{i}", [128, 512], f32)) for i in range(8)]
        BLK, SB_, TB, PVB = BANK[0:3], BANK[3:5], BANK[5:7], BANK[7]
        GAB, UAB, HTB, YAB, SCB = BANK[0:2], BANK[2:4], BANK[4], BANK[5], BANK[6:8]

        def sem(name):
            return ctx.enter_context(nc.semaphore(name))

        const_in = sem("const_in")
        x_in = sem("x_in")
        out_written = sem("out_written")
        blk_ready = sem("blk_ready")
        act_evicted = sem("act_evicted")
        dve_evicted = sem("dve_evicted")
        split_hi = sem("split_hi")
        split_lo = sem("split_lo")
        cond_tanh = sem("cond_tanh")
        cs_ready = sem("cs_ready")
        mod_ready = sem("mod_ready")
        gt2_in = sem("gt2_in")
        sq_ready = sem("sq_ready")
        var_ready = sem("var_ready")
        std_ready = sem("std_ready")
        xn_ready = sem("xn_ready")
        ht_ready = sem("ht_ready")
        qk_hi = sem("qk_hi")
        qk_ready = sem("qk_ready")
        bias_in = sem("bias_in")
        bias_ready = sem("bias_ready")
        s_ready = sem("s_ready")
        max_ready = sem("max_ready")
        exp_ready = sem("exp_ready")
        norm_ready = sem("norm_ready")
        turn_ready = sem("turn_ready")
        pt_ready = sem("pt_ready")
        pv_ready = sem("pv_ready")
        o_hi = sem("o_hi")
        o_ready = sem("o_ready")
        mrg_ready = sem("mrg_ready")
        ml_ready = sem("ml_ready")
        aff_exp = sem("aff_exp")
        rpb_in = sem("rpb_in")
        rpb_tiled = sem("rpb_tiled")
        rpb_saved = sem("rpb_saved")
        aff_ready = sem("aff_ready")
        code_ready = sem("code_ready")
        sel_ready = sem("sel_ready")
        gate_sel = sem("gate_sel")
        xe_ready = sem("xe_ready")
        tanh_ready = sem("tanh_ready")
        silu_ready = sem("silu_ready")
        hid_ready = sem("hid_ready")
        hid_turned = sem("hid_turned")
        hidt_ready = sem("hidt_ready")
        ye_act = sem("ye_act")
        ye_dve = sem("ye_dve")
        stb_ready = sem("stb_ready")
        sc_ready = sem("sc_ready")
        sc_evicted = sem("sc_evicted")
        x_added = sem("x_added")
        gf_in = sem("gf_in")
        dve_chain = sem("dve_chain")
        act_chain = sem("act_chain")
        zeroed = sem("zeroed")
        sem_named = {"dve_evicted": dve_evicted, "qk_ready": qk_ready, "mrg_ready": mrg_ready}
        w_in = [sem(f"w_in{j}") for j in range(NSLOT)]
        chunk_used = [sem(f"chunk_used{j}") for j in range(NSLOT)]
        USED0 = [1, 1, 1, 2, 1, 1]
        HID0 = TURN0 = YE0 = SC0 = X0 = 1
        EV0 = 2
        NS = [2] * (DEPTH - 1) + [1]
        SPG = [4 * n for n in NS]
        SCB0 = [4 * sum(SPG[:l]) for l in range(DEPTH + 1)]

        def released(t):
            return (dve_evicted, t.dve) if t.dve else (act_evicted, t.act)

        def source(ref):
            name, i, c0, n = ref
            a = A[name]
            if name == "w_branch":
                a = a.rearrange("l b k n -> (l b) k n")
            return a[i, :, c0:c0 + n].rearrange("(k p) n -> p k n", p=128)

        def place(chunk_slot, at_, shape):
            return ring[chunk_slot][:, at_:at_ + shape[0] * shape[1]].rearrange("p (k n) -> p k n", k=shape[0])

        def bcast_rows(row):
            return bass.AP(tensor=row.tensor, offset=row.offset, ap=[[0, 128]] + list(row.ap))

        NCONST = 10
        block = ctx.enter_context(nc.Block())

        @block.sync
        def _(sp):
            sp.dma_start(CONST[:], A["consts"]).then_inc(const_in, 16)
            r96 = A["b_ada"].rearrange("l (r p) -> (l r) p", p=128)
            sp.dma_start(ROWS[0:96, 0, :], r96).then_inc(const_in, 16)
            sp.dma_start(ROWS[96:112, 0, :], A["g_mix"].rearrange("l (r p) -> (l r) p", p=128)).then_inc(const_in, 16)
            sp.dma_start(ROWS[112:128, 0, :], A["g_ffn"].rearrange("l (r p) -> (l r) p", p=128)).then_inc(const_in, 16)
            sp.dma_start(ROWS[0:8, 1, :], A["c"].rearrange("o (r p) -> (o r) p", p=128)).then_inc(const_in, 16)
            sp.dma_start(ROWS[8:16, 1, :], A["c_ctx"].rearrange("(r p) -> r p", p=128)).then_inc(const_in, 16)
            sp.dma_start(ROWS[16:NROW2, 1, :], A["conv_w"].rearrange("l t (r p) -> (l t r) p", p=128)).then_inc(const_in, 16)
            for l in range(DEPTH):
                sp.dma_start(WR[:, l, :, :], A["w_router"][l].rearrange("(k p) e -> p k e", p=128)).then_inc(const_in, 16)
            sp.dma_start(SINK[:].rearrange("p l h -> p (l h)"),
                         bcast_rows(A["sw_sink"].rearrange("l h -> (l h)"))).then_inc(const_in, 16)
            first = True
            for l in range(DEPTH + 1):
                for s in P.steps[l]:
                    if s.kind == "load":
                        c = s.chunk
                        if c.before is not None:
                            o = c.before
                            if o.expert is not None:
                                sp.wait_ge(chunk_used[o.slot], USED0[o.slot] + NE * (o.expert + 1))
                            elif o.used_tile:
                                sp.wait_ge(blk_ready, o.used_tile)
                            else:
                                sp.wait_ge(split_lo, o.split_end)
                        for at_, shape, ref in c.parts:
                            sp.dma_start(place(c.slot, at_, shape), source(ref)).then_inc(w_in[c.slot], 16)
                        if first:
                            first = False
                            sp.dma_start(X[:, 0:2, :], A["x"].rearrange("o (t p) d -> p (o t) d", p=128)).then_inc(x_in, 16)
                            sp.dma_start(X[:, 2:4, :], A["ctx"].rearrange("o (t p) d -> p (o t) d", p=128)).then_inc(x_in, 16)
                    elif s.kind == "gt2_bias":
                        sp.wait_ge(pv_ready, s.sets)
                        row = A["b_ada"][s.l, GT2V * D:(GT2V + 1) * D]
                        for q in range(2):
                            sp.dma_start(GT2[:, q, :], bcast_rows(row)).then_inc(gt2_in, 16)
                    elif s.kind == "moe":
                        mats = (A["w_exp_gate"][l], A["w_exp_up"][l], A["w_exp_down"][l])

                        def expert_chunk(e, j):
                            return mats[j // 2][e, 512 * (j % 2):512 * (j % 2 + 1), :].rearrange("a (k p) n -> p (a k) n", p=128)

                        for j in range(NSLOT):
                            if j < 2:
                                o = s.before[j]
                                if o.used_tile:
                                    sp.wait_ge(blk_ready, o.used_tile)
                                else:
                                    sp.wait_ge(split_lo, o.split_end)
                            else:
                                sp.wait_ge(blk_ready, s.c_tile if j < 4 else s.d_tile)
                            sp.dma_start(place(j, 0, (4, D)), expert_chunk(slice(0, 1), j)).then_inc(w_in[j], 16)
                        with sp.Fori(1, NE) as e:
                            for j in range(NSLOT):
                                sp.wait_ge(chunk_used[j], e + (USED0[j] + NE * l))
                                sp.dma_start(place(j, 0, (4, D)), expert_chunk(bass.ds(e, 1), j)).then_inc(w_in[j], 16)
                    elif s.kind == "final":
                        sp.wait_ge(chunk_used[0], USED0[0] + NE * DEPTH)
                        sp.dma_start(GF[:], bcast_rows(A["g_final"])).then_inc(gf_in, 16)
                        sp.wait_ge(x_added, X0 + SCB0[DEPTH] + 2)
                        sp.dma_start(out.rearrange("o (t p) d -> p (o t) d", p=128), XN[:, 0:2, :]).then_inc(out_written, 16)
                        sp.wait_ge(out_written, 16)

        @block.gpsimd
        def _(pool):
            waited_layer = 0
            nbias = 0
            for l in range(DEPTH):
                pool.dma_start(RPB[:, l, :], A["na_rpb"][l].rearrange("h r c -> (h r) c")).then_inc(rpb_in, 16)
            pool.wait_ge(rpb_in, 16 * DEPTH)
            for l in range(DEPTH):
                nc.gpsimd.tensor_copy(RPBT[l][:], RPB[:, l, :].unsqueeze(1).broadcast_to((8 * RPB_R, RPB_REP, RPB_C))).then_inc(rpb_tiled, 1)
                pool.wait_ge(rpb_tiled, l + 1)
                pool.dma_start(tiled[l], RPBT[l][:].rearrange("p a c -> p (a c)")).then_inc(rpb_saved, 16)
            pool.wait_ge(rpb_saved, 16 * DEPTH)
            for l in range(DEPTH):
                for s in P.steps[l]:
                    if s.kind == "bias":
                        x = s.unit
                        if x.bias_before:
                            pool.wait_ge(max_ready, x.bias_before)
                        if l > waited_layer:
                            waited_layer = l
                            pool.wait_ge(x_added, X0 + SCB0[l])
                        h = 2 * x.p + x.hh
                        for rr in range(2):
                            r = 2 * x.qt + rr
                            off = tiled[l].offset + (h * RPB_R + 7 - r) * RPB_REP * RPB_C + 15
                            toeplitz = bass.AP(tensor=tiled[l].tensor, offset=off,
                                               ap=[[RPB_C - 1, GRID_W], [RPB_REP * RPB_C, 4], [1, GRID_W]])
                            pool.dma_start(BIAS[x.bias % 2][64 * rr:64 * rr + 64, :].rearrange("p (r k) -> p r k", r=4),
                                           toeplitz).then_inc(bias_in, 16)
                        nbias += 1
                        if nbias == 1:
                            pool.wait_ge(const_in, 16 * NCONST)
                        pool.wait_ge(bias_in, 32 * nbias)
                        nc.gpsimd.tensor_tensor(BIAS[x.bias % 2][:], BIAS[x.bias % 2][:], NAM, ALU.add).then_inc(bias_ready, 1)
                    elif s.kind == "moe":
                        tw = CAP * s.ns
                        xe = XE[s.ns - 1]
                        pool.wait_ge(act_evicted, s.act)
                        pool.wait_ge(dve_evicted, s.dve)
                        with pool.Fori(0, 4) as g:
                            pool.wait_ge(sc_ready, g * SPG[l] + (SC0 + SCB0[l]))
                            for eo in range(4):
                                pool.wait_ge(chunk_used[3], g * 4 + (USED0[3] + NE * l + eo - 1))
                                nc.gpsimd.tensor_copy(XEB[eo % 2][:, :, 0:tw],
                                                      xe[:, :, bass.ds(g * 4 + eo, 1), :].rearrange("p k a t -> p k (a t)")).then_inc(xe_ready, 1)
                                if eo == 0:
                                    nc.gpsimd.tensor_copy(STB[:, 0:s.ns, :],
                                                          ST[:, bass.ds(g, 1), 0:s.ns, :].rearrange("p a s t -> p (a s) t")).then_inc(stb_ready, 1)

        @block.scalar
        def _(act):
            chain = [0]
            norms = [0]

            def link(ins):
                chain[0] += 1
                ins.then_inc(act_chain, 1)
                act.wait_ge(act_chain, chain[0])

            def norm(s):
                if s.kind == "final" or (s.which == 0 and s.layer > 0):
                    act.wait_ge(x_added, X0 + SCB0[s.layer])
                elif s.which == 0:
                    act.wait_ge(x_in, 32)
                else:
                    act.wait_ge(dve_evicted, s.x_updated)
                for tt in range(s.ntt):
                    last = nc.scalar.activation(XN[:, tt, :], X[:, tt, :], ACT.Square, accum_out=SS[:, tt:tt + 1])
                last.then_inc(sq_ready, 1)
                norms[0] += 1
                act.wait_ge(var_ready, norms[0])
                nc.scalar.activation(SD[:, 0:s.ntt], VV[:, 0:s.ntt], ACT.Sqrt).then_inc(std_ready, 1)

            for l in range(DEPTH + 1):
                for s in P.steps[l]:
                    kind = s.kind
                    if kind == "pre":
                        act.wait_ge(blk_ready, s.tile.ready)
                        link(nc.scalar.copy(COLS[:], BLK[s.tile.bank][:, 0:128 + NROW2]))
                        nc.scalar.activation(TC, COLS[:, 128:144], ACT.Tanh, scale=0.5).then_inc(act_evicted, 1)
                    elif kind == "split":
                        b = s.blk
                        act.wait_ge(w_in[b.chunk.slot], b.chunk.arrived)
                        if b.b >= NWS:
                            act.wait_ge(blk_ready, P.blocks[b.b - NWS].tile.ready)
                        w = place(b.chunk.slot, b.at, (b.kk, b.width))[:, :, b.col:b.col + 128]
                        nc.scalar.copy(WH[b.b % NWS][:, 0:b.kk, :], w).then_inc(split_hi, 1)
                    elif kind == "norm":
                        norm(s)
                    elif kind == "trmod":
                        act.wait_ge(blk_ready, s.tile.ready)
                        if s.k == 0:
                            act.wait_ge(mod_ready, s.mods)
                        if s.which == 0 and s.hts > 1:
                            act.wait_ge(ht_ready, s.hts - 1)
                        sh, sc = (SH1, SC1) if s.which == 0 else (SH2, SC2)
                        dst = FT[s.k % 2][:] if s.which == 0 else H2[:, s.k, :]
                        for q in range(s.ntt // 2):
                            last = nc.scalar.activation(dst[:, SEQ * q:SEQ * q + SEQ], BLK[s.tile.bank][:, SEQ * q:SEQ * q + SEQ], ACT.Identity,
                                                        scale=MOD[:, l, sc, s.k, q:q + 1], bias=MOD[:, l, sh, s.k, q:q + 1])
                        last.then_inc(act_evicted, 1)
                    elif kind == "done":
                        b = s.blk
                        if b.out in ("ac", "v", "nq", "nk", "sk", "sq", "gate", "out"):
                            act.wait_ge(blk_ready, b.tile.ready)
                            t = BLK[b.tile.bank]
                        if b.out == "ac":
                            nc.scalar.copy(AC[:, b.i, 0:b.n], t[:, 0:b.n]).then_inc(act_evicted, 1)
                        elif b.out == "v":
                            if l == 0 and b.i == 1:
                                act.wait_ge(rpb_tiled, DEPTH)
                            nc.scalar.copy(VT[b.i % 2][:], t[:]).then_inc(act_evicted, 1)
                        elif b.out == "nq":
                            for hh in range(2):
                                for half in range(2):
                                    last = nc.scalar.activation(dup[b.p % 2][64 * half:64 * half + 64, 0, hh, 0:b.n],
                                                                t[64 * hh:64 * hh + 64, 0:b.n], ACT.Copy, scale=HD ** -0.5)
                            last.then_inc(act_evicted, 1)
                        elif b.out == "nk":
                            for hh in range(2):
                                last = nc.scalar.copy(stk[b.p % 2][64 * hh:64 * hh + 64, hh, 0:b.n], t[64 * hh:64 * hh + 64, 0:b.n])
                            last.then_inc(act_evicted, 1)
                        elif b.out in ("sk", "sq"):
                            if b.rope > 1:
                                act.wait_ge(qk_ready, b.rope - 1)
                            nc.scalar.activation(QT[:, 0:b.n], t[:, 0:b.n], ACT.Copy,
                                                 scale=HD ** -0.5 if b.out == "sq" else 1.0).then_inc(act_evicted, 1)
                        elif b.out == "gate":
                            if b.gt_free:
                                act.wait_ge(sem_named[b.gt_free[0]], b.gt_free[1])
                            nc.scalar.activation(GT[:, 0:b.n], t[:, 0:b.n], ACT.Tanh, scale=0.5).then_inc(act_evicted, 1)
                        elif b.out == "out":
                            act.wait_ge(mod_ready, b.mods)
                            for q in range(b.n // SEQ):
                                last = nc.scalar.activation(YT[b.d % 2][:, SEQ * q:SEQ * q + SEQ], t[:, SEQ * q:SEQ * q + SEQ], ACT.Copy,
                                                            scale=MOD[:, l, GT1, b.d, q:q + 1])
                            last.then_inc(act_evicted, 1)
                    elif kind == "finish" and s.blk.rope:
                        b = s.blk
                        act.wait_ge(dve_evicted, b.rot_tile.dve)
                        if b.out == "sq":
                            for hh in range(2):
                                last = nc.scalar.copy(stk[b.p % 2][64 * hh:64 * hh + 64, hh, 0:b.n], QT[64 * hh:64 * hh + 64, 0:b.n])
                        else:
                            for hh in range(2):
                                for half in range(2):
                                    last = nc.scalar.copy(dup[0][64 * half:64 * half + 64, 0, hh, 0:b.n], QT[64 * hh:64 * hh + 64, 0:b.n])
                        last.then_inc(qk_hi, 1)
                    elif kind == "score":
                        x = s.unit
                        u2 = x.u % 2
                        act.wait_ge(max_ready, x.u + 1)
                        sc, p_ = SB_[u2], PB[u2]
                        if x.qt < 2:
                            nc.scalar.activation(p_[:, 0:SEQ], p_[:, 0:SEQ], ACT.Exp, bias=NM[u2], accum_out=ES[u2][:, 0:1])
                            last = nc.scalar.activation(p_[:, SEQ:TOK], sc[:, SEQ:TOK], ACT.Exp, bias=NM[u2], accum_out=ES[u2][:, 1:2])
                        else:
                            last = nc.scalar.activation(p_[:, 0:CTX], sc[:, 0:CTX], ACT.Exp, bias=NM[u2], accum_out=ES[u2][:, 0:1])
                        if x.br == "sw":
                            last = nc.scalar.activation(ES[u2][:, 2:3], SINK[:, l, 2 * x.p + x.hh:2 * x.p + x.hh + 1], ACT.Exp, bias=NM[u2])
                        last.then_inc(exp_ready, 1)
                    elif kind == "turn":
                        x = s.unit
                        act.wait_ge(turn_ready, x.u + 1)
                        if x.set.pt_before:
                            act.wait_ge(pv_ready, x.set.pt_before)
                        buf, nk = (PTL, 4) if x.set.grp == 0 else (PTC, 2)
                        j = x.qt % 2
                        nc.scalar.copy(buf[:, x.hh, :, 128 * j:128 * j + 128],
                                       TB[x.u % 2][:, 0:128 * nk].rearrange("p (k q) -> p k q", k=nk)).then_inc(pt_ready, 1)
                    elif kind == "pv":
                        st = s.set
                        act.wait_ge(pv_ready, st.set + 1)
                        ob = 1 if st.br == "na" else 0
                        nc.scalar.copy(OH[ob][:, st.p, SEQ * st.grp:SEQ * st.grp + SEQ], PVB[:, 0:SEQ]).then_inc(o_hi, 1)
                    elif kind == "route":
                        act.wait_ge(blk_ready, s.lg.ready)
                        n = SEQ * s.ns
                        nc.scalar.copy(LG[:, 0:n], BLK[s.lg.bank][0:NE, 0:n]).then_inc(act_evicted, 1)
                        act.wait_ge(dve_evicted, s.lt.dve)
                        nc.scalar.activation(AFF[:, :, 0:s.ns, :], AFF[:, :, 0:s.ns, :], ACT.Exp).then_inc(aff_exp, 1)
                    elif kind == "gather" and s.tile.act:
                        act.wait_ge(blk_ready, s.tile.ready)
                        nc.scalar.activation(XE[s.ns - 1][:, s.k, :, CAP * s.s:CAP * s.s + CAP],
                                             BLK[s.tile.bank][:].rearrange("p (e t) -> p e t", e=NE), ACT.Identity,
                                             scale=MOD[:, l, SC2, s.k, s.s:s.s + 1], bias=MOD[:, l, SH2, s.k, s.s:s.s + 1]).then_inc(act_evicted, 1)
                    elif kind == "gates":
                        for q in range(s.ns):
                            t = s.tiles[q][0]
                            act.wait_ge(blk_ready, t.ready)
                            nc.scalar.copy(ST[:, 0:2, q, :], BLK[t.bank][:].rearrange("p (g t) -> p g t", g=2)).then_inc(act_evicted, 1)
                    elif kind == "moe":
                        G = 2 if s.ns == 2 else 4
                        tw, nw = 128 // G, D // G
                        with act.Fori(0, 4) as g:
                            for eo in range(4):
                                e0 = NE * l + eo
                                act.wait_ge(chunk_used[1], g * 4 + (USED0[1] + e0 + 1))
                                act.wait_ge(hid_ready, g * 4 + (HID0 + e0))
                                nc.scalar.activation(TH[:, 0:nw], GAB[eo % 2][:, 0:nw], ACT.Tanh, scale=0.5).then_inc(tanh_ready, 1)
                                act.wait_ge(hid_turned, g * 4 + (TURN0 + e0 + 1))
                                nc.scalar.activation(HIDT[:, :, 0:tw].rearrange("p (h c) t -> p c h t", h=G),
                                                     HTB[:, 0:8 * tw].rearrange("p (c h t) -> p c h t", h=G, t=tw), ACT.Copy, scale=0.5).then_inc(hidt_ready, 1)
                                act.wait_ge(chunk_used[5], g * 4 + (USED0[5] + e0 + 1))
                                if G == 2:
                                    for q in range(2):
                                        last = nc.scalar.copy(YE[32 * eo:32 * eo + 32, q, 0:nw], YAB[32 * q:32 * q + 32, 0:nw])
                                else:
                                    for q in range(2):
                                        last = nc.scalar.copy(YE[32 * eo:32 * eo + 32, 0, nw * q:nw * q + nw], YAB[32 * q:32 * q + 32, 0:nw])
                                last.then_inc(ye_act, 1)
                    elif kind == "final":
                        s.ntt = 2
                        norm(s)

        @block.vector
        def _(dve):
            chain = [0]
            counts = dict(norm=0, xn=0, gt2=0)

            def link(ins):
                chain[0] += 1
                ins.then_inc(dve_chain, 1)
                dve.wait_ge(dve_chain, chain[0])

            def norm(ntt):
                counts["norm"] += 1
                n = counts["norm"]
                dve.wait_ge(sq_ready, n)
                nc.vector.tensor_scalar(VV[:, 0:ntt], SS[:, 0:ntt], 1.0 / D, EPS, ALU.mult, ALU.add).then_inc(var_ready, 1)
                dve.wait_ge(var_ready, n)
                dve.wait_ge(std_ready, n)
                link(nc.vector.reciprocal(RS[:, 0:ntt], SD[:, 0:ntt]))
                link(nc.vector.tensor_tensor(NW[:, 0:ntt], RS[:, 0:ntt], RS[:, 0:ntt], ALU.mult))
                link(nc.vector.tensor_tensor(NW[:, 0:ntt], NW[:, 0:ntt], VV[:, 0:ntt], ALU.mult))
                link(nc.vector.tensor_scalar(NW[:, 0:ntt], NW[:, 0:ntt], -0.5, 1.5, ALU.mult, ALU.add))
                link(nc.vector.tensor_tensor(RS[:, 0:ntt], RS[:, 0:ntt], NW[:, 0:ntt], ALU.mult))

            for i, (sem_, n) in enumerate([(chunk_used[j], USED0[j]) for j in range(NSLOT)]
                            + [(hid_ready, HID0), (hid_turned, TURN0), (ye_act, YE0), (ye_dve, YE0),
                               (sc_ready, SC0), (sc_evicted, EV0), (x_added, X0)]):
                nc.vector.memset(PRIME[:, i:i + 1], 0.0).then_inc(sem_, n)

            for l in range(DEPTH + 1):
                for s in P.steps[l]:
                    kind = s.kind
                    if kind == "pre":
                        link(nc.vector.memset(CS[:], 0.0))
                        dve.wait_ge(act_evicted, s.tile.act)
                        link(nc.vector.scalar_tensor_tensor(T2, TC, 1.0, COLS[:, 128:144], ALU.add, ALU.mult))
                        nc.vector.tensor_scalar(CS[:, :, 0:2].rearrange("p k s -> p s k"), T2.rearrange("p (s k) -> p s k", s=2),
                                                0.5, None, ALU.mult).then_inc(cs_ready, 1)
                    elif kind == "split":
                        b = s.blk
                        dve.wait_ge(split_hi, b.b + 1)
                        w = place(b.chunk.slot, b.at, (b.kk, b.width))[:, :, b.col:b.col + 128]
                        nc.vector.tensor_tensor(WL[b.b % NWS][:, 0:b.kk, :], w, WH[b.b % NWS][:, 0:b.kk, :].bitcast(f32),
                                                ALU.subtract).then_inc(split_lo, 1)
                    elif kind == "ada":
                        dve.wait_ge(blk_ready, s.tile.ready)
                        nc.vector.tensor_copy(MB[:], BLK[s.tile.bank][:]).then_inc(dve_evicted, 1)
                    elif kind == "ada2":
                        if s.v == GT2V:
                            for q in range(2):
                                if counts["gt2"] < 32 * (s.l + 1):
                                    counts["gt2"] = 32 * (s.l + 1)
                                    dve.wait_ge(gt2_in, counts["gt2"])
                                dve.wait_ge(blk_ready, s.out[q].ready)
                                g2 = GT2[:, q, 512 * s.half:512 * s.half + 512]
                                nc.vector.tensor_tensor(g2, BLK[s.out[q].bank][:], g2, ALU.add).then_inc(dve_evicted, 1)
                        else:
                            dve.wait_ge(blk_ready, s.out[0].ready)
                            turned = BLK[s.out[0].bank][:].rearrange("p (k j c) -> p k c j", k=4, j=4)[:, :, 0:2, :]
                            nc.vector.tensor_reduce(RED, turned, AX.X, ALU.add).then_inc(dve_evicted, 1)
                            dve.wait_ge(dve_evicted, s.out[0].dve)
                            m = MOD[:, s.l, s.v, 4 * s.half:4 * s.half + 4, :]
                            c0 = 48 * s.l + 8 * s.v + 4 * s.half
                            bias = COLS[:, c0:c0 + 4].unsqueeze(2).broadcast_to((128, 4, 2))
                            add = nc.vector.tensor_tensor(m, RED, bias, ALU.add)
                            if s.v in (SH1, SH2):
                                add.then_inc(mod_ready, 1)
                            elif s.v == GT1:
                                link(add)
                                nc.vector.tensor_scalar(m, m, 0.5, None, ALU.mult).then_inc(mod_ready, 1)
                            else:
                                link(add)
                                c0 = (96 if s.v == SC1 else 112) + 8 * s.l + 4 * s.half
                                g = COLS[:, c0:c0 + 4].unsqueeze(2).broadcast_to((128, 4, 2))
                                link(nc.vector.tensor_scalar(m, m, 1.0, None, ALU.add))
                                nc.vector.tensor_tensor(m, m, g, ALU.mult).then_inc(mod_ready, 1)
                    elif kind == "norm":
                        norm(s.ntt)
                        for tt in range(s.ntt):
                            nc.vector.tensor_scalar(XN[:, tt, :], X[:, tt, :], RS[:, tt:tt + 1], None, ALU.mult).then_inc(xn_ready, 1)
                    elif kind == "trmod" and s.which == 0:
                        dve.wait_ge(act_evicted, s.tile.act)
                        link(nc.vector.tensor_copy(HH[:, s.k, :], FT[s.k % 2][:]))
                        nc.vector.tensor_tensor(HL[:, s.k, :], FT[s.k % 2][:], HH[:, s.k, :].bitcast(f32), ALU.subtract).then_inc(ht_ready, 1)
                    elif kind == "done":
                        b = s.blk
                        if b.out in ("ax", "ab", "nq", "nk", "br"):
                            dve.wait_ge(blk_ready, b.tile.ready)
                            t = BLK[b.tile.bank]
                        ns = b.n // SEQ
                        if b.out == "ax":
                            if b.i == 0:
                                link(nc.vector.memset(U[:].rearrange("p i s t -> p (i s) t")[:, :, 0:1], 0.0))
                                link(nc.vector.memset(U[:].rearrange("p i s t -> p (i s) t")[:, :, SEQ + 1:SEQ + 2], 0.0))
                            dve.wait_ge(act_evicted, b.ac_tile.act)
                            nc.vector.tensor_tensor(U[:, b.i, 0:ns, 1:SEQ + 1], t[:, 0:b.n].rearrange("p (s t) -> p s t", s=ns),
                                                    AC[:, b.i, 0:b.n].rearrange("p (s t) -> p s t", s=ns), ALU.mult).then_inc(dve_evicted, 1)
                        elif b.out == "ab":
                            if b.i == 0:
                                dve.wait_ge(dve_evicted, b.tile.dve - 1)
                            else:
                                dve.wait_ge(o_ready, b.o_ready - 1)
                            tap = [COLS[:, 144 + 12 * l + 4 * k + b.i:145 + 12 * l + 4 * k + b.i] for k in range(3)]
                            ct = CT[:, 0:ns, :]
                            link(nc.vector.tensor_scalar(ct, U[:, b.i, 0:ns, 0:SEQ], tap[0], None, ALU.mult))
                            link(nc.vector.scalar_tensor_tensor(ct, U[:, b.i, 0:ns, 1:SEQ + 1], tap[1], ct, ALU.mult, ALU.add))
                            link(nc.vector.scalar_tensor_tensor(ct, U[:, b.i, 0:ns, 2:SEQ + 2], tap[2], ct, ALU.mult, ALU.add))
                            nc.vector.tensor_tensor(ct, ct, t[:, 0:b.n].rearrange("p (s t) -> p s t", s=ns), ALU.mult).then_inc(dve_evicted, 1)
                            dve.wait_ge(dve_evicted, b.tile.dve)
                            oh = OH[0][:, b.i, 0:b.n].rearrange("p (s t) -> p s t", s=ns)
                            ol = OL[0][:, b.i, 0:b.n].rearrange("p (s t) -> p s t", s=ns)
                            link(nc.vector.tensor_copy(oh, ct))
                            nc.vector.tensor_tensor(ol, ct, oh.bitcast(f32), ALU.subtract).then_inc(o_ready, 1)
                        elif b.out == "nq":
                            dve.wait_ge(act_evicted, b.tile.act)
                            for hh in range(2):
                                own = slice(64 * hh, 64 * hh + 64)
                                for half in range(2):
                                    last = nc.vector.scalar_tensor_tensor(dup[b.p % 2][64 * half:64 * half + 64, 1, hh, 0:b.n], t[own, 0:b.n], HD ** -0.5,
                                                                          dup[b.p % 2][own, 0, hh, 0:b.n].bitcast(f32), ALU.mult, ALU.subtract)
                            last.then_inc(dve_evicted, 1)
                        elif b.out == "nk":
                            dve.wait_ge(act_evicted, b.tile.act)
                            for hh in range(2):
                                own, other = slice(64 * hh, 64 * hh + 64), slice(64 - 64 * hh, 128 - 64 * hh)
                                last = nc.vector.tensor_tensor(stk[b.p % 2][other, hh, 0:b.n], t[own, 0:b.n],
                                                               stk[b.p % 2][own, hh, 0:b.n].bitcast(f32), ALU.subtract)
                            last.then_inc(dve_evicted, 1)
                        elif b.out == "br":
                            dve.wait_ge(act_evicted, b.gate.tile.act)
                            g, m = GT[:, 0:b.n], MRG[:, b.d, 0:b.n]
                            if b.i == 0:
                                nc.vector.scalar_tensor_tensor(m, g, 1.0, t[:, 0:b.n], ALU.add, ALU.mult).then_inc(dve_evicted, 1)
                            else:
                                nc.vector.scalar_tensor_tensor(g, g, 1.0, t[:, 0:b.n], ALU.add, ALU.mult).then_inc(dve_evicted, 1)
                                dve.wait_ge(dve_evicted, b.tile.dve)
                                nc.vector.tensor_tensor(m, m, g, ALU.add).then_inc(mrg_ready, 1)
                                if b.i == 2:
                                    dve.wait_ge(mrg_ready, b.sum)
                                    link(nc.vector.tensor_copy(MH[:, b.d, 0:b.n], m))
                                    nc.vector.tensor_tensor(ML[:, b.d, 0:b.n], m, MH[:, b.d, 0:b.n].bitcast(f32), ALU.subtract).then_inc(ml_ready, 1)
                    elif kind == "finish":
                        b = s.blk
                        ns = b.n // SEQ
                        if b.out == "v":
                            dve.wait_ge(blk_ready, b.out_tile.ready)
                            dst = V[:, :, 128 * b.i:128 * b.i + 128] if b.i < KB else VS[:]
                            nc.vector.tensor_copy(dst, BLK[b.out_tile.bank][:].rearrange("p (t c) -> p t c", t=NTT)).then_inc(dve_evicted, 1)
                        elif b.out in ("sk", "sq"):
                            dve.wait_ge(blk_ready, b.rot_tile.ready)
                            r = BLK[b.rot_tile.bank]
                            nc.vector.tensor_tensor(r[:, SEQ:2 * SEQ], r[:, 0:SEQ], ROPE[:, 1, :], ALU.mult)
                            link(nc.vector.tensor_tensor(QT[:, 0:SEQ], QT[:, 0:SEQ], ROPE[:, 0, :], ALU.mult))
                            nc.vector.tensor_tensor(QT[:, 0:SEQ], QT[:, 0:SEQ], r[:, SEQ:2 * SEQ], ALU.add).then_inc(dve_evicted, 1)
                            dve.wait_ge(qk_hi, b.rope)
                            for hh in range(2):
                                own, other = slice(64 * hh, 64 * hh + 64), slice(64 - 64 * hh, 128 - 64 * hh)
                                if b.out == "sq":
                                    last = nc.vector.tensor_tensor(stk[b.p % 2][other, hh, 0:b.n], QT[own, 0:b.n],
                                                                   stk[b.p % 2][own, hh, 0:b.n].bitcast(f32), ALU.subtract)
                                else:
                                    for half in range(2):
                                        last = nc.vector.tensor_tensor(dup[0][64 * half:64 * half + 64, 1, hh, 0:b.n], QT[own, 0:b.n],
                                                                       dup[0][own, 0, hh, 0:b.n].bitcast(f32), ALU.subtract)
                            last.then_inc(qk_ready, 1)
                        elif b.out == "out":
                            dve.wait_ge(blk_ready, b.out_tile.ready)
                            xs = X[:, 0:2 * ns, 128 * b.d:128 * b.d + 128]
                            nc.vector.tensor_tensor(xs, xs, BLK[b.out_tile.bank][:, 0:b.n].rearrange("p (t c) -> p t c", t=2 * ns), ALU.add).then_inc(dve_evicted, 1)
                    elif kind == "score":
                        x = s.unit
                        u2 = x.u % 2
                        sc, p_ = SB_[u2], PB[u2]
                        dve.wait_ge(s_ready, x.u + 1)
                        sink = SINK[:, l, 2 * x.p + x.hh:2 * x.p + x.hh + 1]
                        if x.qt < 2:
                            if x.u >= 2:
                                dve.wait_ge(turn_ready, x.u - 1)
                            if x.bias:
                                dve.wait_ge(bias_ready, x.bias)
                            add = BIAS[x.bias % 2][:] if x.bias else SWM[:, x.qt, :]
                            nc.vector.tensor_tensor_reduce(p_[:, 0:SEQ], sc[:, 0:SEQ], add, 1.0, sink if x.br == "sw" else -3e38,
                                                           ALU.add, ALU.max, MX[u2][:, 0:1])
                            link(nc.vector.tensor_reduce(MX[u2][:, 1:2], sc[:, SEQ:TOK], AX.X, ALU.max))
                            nc.vector.tensor_reduce(NM[u2], MX[u2], AX.X, ALU.max, negate=True).then_inc(max_ready, 1)
                        elif x.br == "na":
                            if x.u >= 2:
                                dve.wait_ge(turn_ready, x.u - 1)
                            nc.vector.tensor_reduce(NM[u2], sc[:, 0:CTX], AX.X, ALU.max, negate=True).then_inc(max_ready, 1)
                        else:
                            if x.u >= 2:
                                dve.wait_ge(turn_ready, x.u - 1)
                            link(nc.vector.tensor_reduce(MX[u2][:, 0:1], sc[:, 0:CTX], AX.X, ALU.max))
                            nc.vector.tensor_scalar(NM[u2], MX[u2][:, 0:1], sink, -1.0, ALU.max, ALU.mult).then_inc(max_ready, 1)
                    elif kind == "normalise":
                        x = s.unit
                        u2 = x.u % 2
                        dve.wait_ge(exp_ready, x.u + 1)
                        es, n = ES[u2], x.nk
                        if x.qt < 2 and x.br == "na":
                            link(nc.vector.tensor_tensor(RSM[u2], es[:, 0:1], es[:, 1:2], ALU.add))
                        elif x.qt < 2:
                            link(nc.vector.tensor_reduce(RSM[u2], es[:, 0:3], AX.X, ALU.add))
                        elif x.br == "sw":
                            link(nc.vector.tensor_tensor(RSM[u2], es[:, 0:1], es[:, 2:3], ALU.add))
                        else:
                            link(nc.vector.tensor_copy(RSM[u2], es[:, 0:1]))
                        link(nc.vector.reciprocal(RSM[u2], RSM[u2]))
                        nc.vector.tensor_scalar(PB[u2][:, 0:n], PB[u2][:, 0:n], RSM[u2], None, ALU.mult).then_inc(norm_ready, 1)
                    elif kind == "pv":
                        st = s.set
                        ob = 1 if st.br == "na" else 0
                        dve.wait_ge(o_hi, st.set + 1)
                        cols = slice(SEQ * st.grp, SEQ * st.grp + SEQ)
                        nc.vector.tensor_tensor(OL[ob][:, st.p, cols], PVB[:, 0:SEQ], OH[ob][:, st.p, cols].bitcast(f32), ALU.subtract).then_inc(o_ready, 1)
                    elif kind == "route":
                        ns, ntt = s.ns, 2 * s.ns
                        lt = BLK[s.lt.bank][:, 0:NE * ntt].rearrange("p (t e) -> p t e", e=NE)
                        dve.wait_ge(blk_ready, s.lt.ready)
                        link(nc.vector.tensor_reduce(RMX[:, 0:ntt], lt, AX.X, ALU.max, negate=True))
                        aff = AFF[:, :, 0:ns, :]
                        nc.vector.tensor_tensor(aff.rearrange("p j s e -> p s j e"), lt.rearrange("p (s j) e -> p s j e", j=2),
                                                RMX[:, 0:ntt].rearrange("p (s j) -> p s j", j=2).unsqueeze(3).broadcast_to((128, ns, 2, NE)),
                                                ALU.add).then_inc(dve_evicted, 1)
                        dve.wait_ge(aff_exp, l + 1)
                        rs = RSUM[:, 0:ntt].rearrange("p (j s) -> p j s", j=2)
                        link(nc.vector.tensor_reduce(rs, aff, AX.X, ALU.add))
                        link(nc.vector.reciprocal(RSUM[:, 0:ntt], RSUM[:, 0:ntt]))
                        nc.vector.tensor_tensor(aff, aff, rs.unsqueeze(3).broadcast_to((128, 2, ns, NE)), ALU.mult).then_inc(aff_ready, 1)
                        R = NE * ns
                        dve.wait_ge(blk_ready, s.at.ready)
                        nc.vector.tensor_copy(WK[0:R, :], BLK[s.at.bank][0:R, 0:SEQ]).then_inc(dve_evicted, 1)
                        dve.wait_ge(dve_evicted, s.at.dve)
                        for _ in range(CAP // 8):
                            link(nc.vector.max(M8[0:R, :], WK[0:R, :]))
                            link(nc.vector.match_replace(WK[0:R, :], M8[0:R, :], WK[0:R, :], -1.0))
                        link(nc.vector.tensor_scalar(MASK[0:R, :], WK[0:R, :], 0.0, None, ALU.is_lt))
                        link(nc.vector.tensor_tensor_scan(CUM[0:R, :], MASK[0:R, :], MASK[0:R, :], 0.0, ALU.add, ALU.bypass))
                        nc.vector.tensor_tensor(CODE[0:R, :], CUM[0:R, :], MASK[0:R, :], ALU.mult).then_inc(code_ready, 1)
                        dve.wait_ge(blk_ready, s.code.ready)
                        nc.vector.tensor_copy(CODT[:, :, 0:ns, :].rearrange("p j s e -> p j (s e)"),
                                              BLK[s.code.bank][:, 0:64].rearrange("p (j r) -> p j r", j=2)[:, :, 0:R]).then_inc(dve_evicted, 1)
                        dve.wait_ge(dve_evicted, s.code.dve)
                        for j in range(2):
                            for q in range(ns):
                                last = nc.vector.tensor_tensor(SELT[:, j, q, :, :], CODT[:, j, q, :].unsqueeze(2).broadcast_to((128, NE, CAP)),
                                                               SLOTS.unsqueeze(1).broadcast_to((128, NE, CAP)), ALU.is_equal)
                        last.then_inc(sel_ready, 1)
                    elif kind == "gather" and s.tile.dve:
                        dve.wait_ge(blk_ready, s.tile.ready)
                        nc.vector.tensor_scalar(XE[s.ns - 1][:, s.k, :, CAP * s.s:CAP * s.s + CAP],
                                                BLK[s.tile.bank][:].rearrange("p (e t) -> p e t", e=NE),
                                                MOD[:, l, SC2, s.k, s.s:s.s + 1], MOD[:, l, SH2, s.k, s.s:s.s + 1],
                                                ALU.mult, ALU.add).then_inc(dve_evicted, 1)
                    elif kind == "gates":
                        dve.wait_ge(blk_ready, s.tiles[0][0].ready - 1)
                        dve.wait_ge(aff_ready, l + 1)
                        for j in range(2):
                            for q in range(s.ns):
                                last = nc.vector.tensor_tensor(SELT[:, j, q, :, :], SELT[:, j, q, :, :],
                                                               AFF[:, j, q, :].unsqueeze(2).broadcast_to((128, NE, CAP)), ALU.mult)
                        last.then_inc(gate_sel, 1)
                        for q in range(s.ns):
                            t = s.tiles[q][1]
                            dve.wait_ge(blk_ready, t.ready)
                            nc.vector.tensor_copy(ST[:, 2:4, q, :], BLK[t.bank][:].rearrange("p (g t) -> p g t", g=2)).then_inc(dve_evicted, 1)
                    elif kind == "moe":
                        G = 2 if s.ns == 2 else 4
                        nw = D // G
                        spg, sc0 = SPG[l], SCB0[l]
                        with dve.Fori(0, 4) as g:
                            for eo in range(4):
                                e0 = NE * l + eo
                                dve.wait_ge(tanh_ready, g * 4 + (e0 + 1))
                                nc.vector.scalar_tensor_tensor(TH[:, 0:nw], TH[:, 0:nw], 1.0, GAB[eo % 2][:, 0:nw], ALU.add, ALU.mult).then_inc(silu_ready, 1)
                                dve.wait_ge(silu_ready, g * 4 + (e0 + 1))
                                dve.wait_ge(chunk_used[3], g * 4 + (USED0[3] + e0 + 1))
                                dve.wait_ge(hid_turned, g * 4 + (TURN0 + e0))
                                nc.vector.tensor_tensor(HID[:, 0:nw], TH[:, 0:nw], UAB[eo % 2][:, 0:nw], ALU.mult).then_inc(hid_ready, 1)
                                dve.wait_ge(chunk_used[5], g * 4 + (USED0[5] + e0 + 1))
                                for q in range(2):
                                    if G == 2:
                                        last = nc.vector.tensor_copy(YE[32 * eo:32 * eo + 32, q, nw:2 * nw], YAB[64 + 32 * q:96 + 32 * q, 0:nw])
                                    else:
                                        last = nc.vector.tensor_copy(YE[32 * eo:32 * eo + 32, 0, nw * (2 + q):nw * (3 + q)], YAB[64 + 32 * q:96 + 32 * q, 0:nw])
                                last.then_inc(ye_dve, 1)
                            i = 0
                            for q in range(s.ns):
                                for j in range(2):
                                    for h in range(2):
                                        dve.wait_ge(sc_ready, g * spg + (SC0 + sc0 + i + 1))
                                        dve.wait_ge(x_added, g * spg + (X0 + sc0 + i))
                                        nc.vector.tensor_tensor(TMP[:], SCB[i % 2][:], GT2[:, q, 512 * h:512 * h + 512], ALU.mult).then_inc(sc_evicted, 1)
                                        dve.wait_ge(sc_evicted, g * spg + (EV0 + sc0 + i + 1))
                                        xs = X[:, 2 * q + j, 512 * h:512 * h + 512]
                                        nc.vector.tensor_tensor(xs, xs, TMP[:], ALU.add).then_inc(x_added, 1)
                                        i += 1
                    elif kind == "final":
                        norm(2)
                        dve.wait_ge(gf_in, 16)
                        for tt in range(2):
                            nc.vector.scalar_tensor_tensor(XN[:, tt, :], X[:, tt, :], RS[:, tt:tt + 1], GF[:], ALU.mult, ALU.mult).then_inc(x_added, 1)

        @block.tensor
        def _(pe):
            mm = nc.tensor.matmul

            def open_tile(t):
                if t.before is not None:
                    sem_, v = released(t.before)
                    pe.wait_ge(sem_, v)
                return BLK[t.bank]

            xn = 0
            for l in range(DEPTH):
                first_block = True
                for s in P.steps[l]:
                    kind = s.kind
                    if kind == "pre":
                        pe.wait_ge(const_in, 16 * NCONST)
                        t = open_tile(s.tile)
                        nc.tensor.transpose(t[:, 0:128], ROWS[:, 0, :], IDENT)
                        nc.tensor.transpose(t[:, 128:128 + NROW2], ROWS[0:NROW2, 1, :], IDENT[0:NROW2, 0:NROW2]).then_inc(blk_ready, 1)
                        pe.wait_ge(cs_ready, 1)
                    elif kind == "ada":
                        t = open_tile(s.tile)
                        pe.wait_ge(w_in[s.chunk.slot], s.chunk.arrived)
                        w = place(s.chunk.slot, 0, (8, 512))
                        for kk in range(2):
                            for j in range(4):
                                last = mm(t[32 * j:32 * j + 32, :], CS[:, 2 * j + kk, :], w[:, 2 * j + kk, :], start=kk == 0, stop=kk == 1,
                                          tile_position=(0, 32 * j))
                        last.then_inc(blk_ready, 1)
                    elif kind == "ada2":
                        pe.wait_ge(dve_evicted, s.tile.dve)
                        if s.v == GT2V:
                            for q in range(2):
                                t = open_tile(s.out[q])
                                mm(t[:], SELB[:, q, :], MB[:], start=True, stop=True).then_inc(blk_ready, 1)
                        else:
                            t = open_tile(s.out[0])
                            for k in range(4):
                                last = nc.tensor.transpose(t[:, 128 * k:128 * k + 128], MB[:, 128 * k:128 * k + 128], IDENT)
                            last.then_inc(blk_ready, 1)
                    elif kind == "norm":
                        xn += s.ntt
                    elif kind == "trmod":
                        if s.k == 0:
                            pe.wait_ge(xn_ready, xn)
                        t = open_tile(s.tile)
                        for tt in range(s.ntt):
                            last = nc.tensor.transpose(t[:, 128 * tt:128 * tt + 128], XN[:, tt, 128 * s.k:128 * s.k + 128], IDENT)
                        last.then_inc(blk_ready, 1)
                    elif kind == "k":
                        b, k = s.blk, s.k
                        if k == 0:
                            open_tile(b.tile)
                            pe.wait_ge(split_lo, b.b + 1)
                            if b.src == "m" and b.d == 0:
                                pe.wait_ge(ml_ready, KD * (l + 1))
                            if b.src[0] == "o":
                                pe.wait_ge(o_ready, b.o_ready_need)
                        if first_block and b.src == "h":
                            pe.wait_ge(ht_ready, KD * l + k + 1)
                            first_block = k < KD - 1
                        hi, lo = {"h": (HH, HL), "m": (MH, ML), "o0": (OH[0], OL[0]), "o1": (OH[1], OL[1]), "o2": (OH[0], OL[0])}[b.src]
                        t, wh, wl = BLK[b.tile.bank][:, 0:b.n], WH[b.b % NWS][:, k, :], WL[b.b % NWS][:, k, :]
                        mm(t, wh, hi[:, k, 0:b.n], start=k == 0, stop=False)
                        mm(t, wh, lo[:, k, 0:b.n], start=False, stop=False)
                        last = mm(t, wl, hi[:, k, 0:b.n], start=False, stop=k == b.kk - 1)
                        if k == b.kk - 1:
                            last.then_inc(blk_ready, 1)
                    elif kind == "finish":
                        b = s.blk
                        if b.out == "v" or b.out == "out":
                            pe.wait_ge(act_evicted, b.tile.act)
                            t, src = open_tile(b.out_tile), VT[b.i % 2] if b.out == "v" else YT[b.d % 2]
                            for tt in range(b.n // 128):
                                last = nc.tensor.transpose(t[:, 128 * tt:128 * tt + 128], src[:, 128 * tt:128 * tt + 128], IDENT)
                            last.then_inc(blk_ready, 1)
                        elif b.out in ("sk", "sq"):
                            pe.wait_ge(act_evicted, b.tile.act)
                            t = open_tile(b.rot_tile)
                            mm(t[:, 0:SEQ], ROT, QT[:, 0:SEQ], start=True, stop=True).then_inc(blk_ready, 1)
                    elif kind == "score":
                        x = s.unit
                        pe.wait_ge(sem_named[x.info.ready[0]], x.info.ready[1])
                        if x.u >= 2:
                            pe.wait_ge(exp_ready, x.u - 1)
                        q0, k0 = 128 * x.qt, TOK - x.nk
                        for part in range(2):
                            if x.br == "na":
                                q, k = dup[x.p % 2][:, part, x.hh, q0:q0 + 128], stk[x.p % 2][:, x.hh, k0:TOK]
                            else:
                                q, k = stk[x.p % 2][:, x.hh, q0:q0 + 128], dup[0][:, part, x.p // 2, k0:TOK]
                            last = mm(SB_[x.u % 2][:, 0:x.nk], q, k, start=part == 0, stop=part == 1)
                        last.then_inc(s_ready, 1)
                    elif kind == "turn":
                        x = s.unit
                        pe.wait_ge(norm_ready, x.u + 1)
                        if x.u >= 2:
                            pe.wait_ge(pt_ready, x.u - 1)
                        for c in range(x.nk // 128):
                            last = nc.tensor.transpose(TB[x.u % 2][:, 128 * c:128 * c + 128], PB[x.u % 2][:, 128 * c:128 * c + 128], IDENT)
                        last.then_inc(turn_ready, 1)
                    elif kind == "pv":
                        st = s.set
                        pe.wait_ge(pt_ready, st.end)
                        pe.wait_ge(dve_evicted, st.v_ready)
                        pe.wait_ge(o_ready, st.o_ready - 1)
                        buf, n = (PTL, 4) if st.grp == 0 else (PTC, 2)
                        for c in range(n):
                            for hh in range(2):
                                kt = c + 4 - n
                                v = V[:, kt, 128 * st.p + 64 * hh:128 * st.p + 64 * hh + 64] if st.br == "na" else \
                                    VS[:, kt, 64 * (st.p // 2):64 * (st.p // 2) + 64]
                                last = mm(PVB[64 * hh:64 * hh + 64, 0:SEQ], v, buf[:, hh, c, :], start=c == 0, stop=c == n - 1,
                                          tile_position=(0, 64 * hh))
                        last.then_inc(pv_ready, 1)
                    elif kind == "route":
                        n, R = SEQ * s.ns, NE * s.ns
                        t = open_tile(s.lg)
                        pe.wait_ge(act_evicted, s.lg.act - 1)
                        for k in range(KD):
                            last = mm(t[0:NE, 0:n], WR[:, l, k, :], H2[:, k, 0:n], start=k == 0, stop=k == KD - 1)
                        last.then_inc(blk_ready, 1)
                        pe.wait_ge(act_evicted, s.lg.act)
                        t = open_tile(s.lt)
                        for tt in range(2 * s.ns):
                            last = nc.tensor.transpose(t[:, NE * tt:NE * tt + NE], LG[:, 128 * tt:128 * tt + 128], IDENT[0:NE, 0:NE])
                        last.then_inc(blk_ready, 1)
                        pe.wait_ge(aff_ready, l + 1)
                        t = open_tile(s.at)
                        for j in range(2):
                            last = nc.tensor.transpose(t[0:R, 128 * j:128 * j + 128], AFF[:, j, 0:s.ns, :].rearrange("p s e -> p (s e)"), IDENT)
                        last.then_inc(blk_ready, 1)
                        pe.wait_ge(code_ready, l + 1)
                        t = open_tile(s.code)
                        for j in range(2):
                            last = nc.tensor.transpose(t[:, 32 * j:32 * j + R], CODE[0:R, 128 * j:128 * j + 128], IDENT[0:R, 0:R])
                        last.then_inc(blk_ready, 1)
                        pe.wait_ge(sel_ready, l + 1)
                    elif kind == "gather":
                        t = open_tile(s.tile)
                        for j in range(2):
                            last = mm(t[:], XN[:, 2 * s.s + j, 128 * s.k:128 * s.k + 128],
                                      SELT[:, j, s.s, :, :].rearrange("p e t -> p (e t)"), start=j == 0, stop=j == 1)
                        last.then_inc(blk_ready, 1)
                    elif kind == "gates":
                        pe.wait_ge(gate_sel, l + 1)
                        for q in range(s.ns):
                            for gp in range(2):
                                t = open_tile(s.tiles[q][gp])
                                for g2 in range(2):
                                    e4 = 4 * (2 * gp + g2)
                                    for j in range(2):
                                        last = nc.tensor.transpose(t[:, 256 * g2 + 128 * j:256 * g2 + 128 * j + 128],
                                                                   SELT[:, j, q, e4:e4 + 4, :].rearrange("p e t -> p (e t)"), IDENT)
                                last.then_inc(blk_ready, 1)
                    elif kind == "moe":
                        G = 2 if s.ns == 2 else 4
                        tw, nw = 128 // G, D // G
                        spg, sc0 = SPG[l], SCB0[l]
                        pe.wait_ge(act_evicted, s.act)
                        pe.wait_ge(dve_evicted, s.dve)
                        with pe.Fori(0, 4) as g:

                            def product(out_bank, stationary, j0, e0, ready=None):
                                for k in range(KD):
                                    j = j0 + k // 4
                                    if k % 4 == 0:
                                        pe.wait_ge(w_in[j], g * 64 + (s.arrive[j] + 16 * (e0 - NE * l + 1)))
                                    w = place(j, 0, (4, D))[:, k % 4, :]
                                    for c in range(G):
                                        last = mm(out_bank[tw * c:tw * c + tw, 0:nw], stationary[:, k, 0:tw], w[:, nw * c:nw * c + nw],
                                                  start=k == 0, stop=k == KD - 1, tile_position=(0, tw * c))
                                    if k % 4 == 3:
                                        last.then_inc(chunk_used[j], 1)

                            for eo in range(4):
                                e0 = NE * l + eo
                                pe.wait_ge(xe_ready, g * 4 + (e0 + 1))
                                product(GAB[eo % 2], XEB[eo % 2], 0, e0)
                                product(UAB[eo % 2], XEB[eo % 2], 2, e0)
                                pe.wait_ge(hid_ready, g * 4 + (HID0 + e0 + 1))
                                for c in range(8 // G):
                                    last = nc.tensor.transpose(HTB[:, 128 * c:128 * c + 128], HID[:, 128 * c:128 * c + 128], IDENT)
                                last.then_inc(hid_turned, 1)
                                pe.wait_ge(hidt_ready, g * 4 + (e0 + 1))
                                pe.wait_ge(ye_act, g * 4 + (YE0 + e0))
                                pe.wait_ge(ye_dve, g * 4 + (YE0 + e0))
                                product(YAB, HIDT, 4, e0)
                            pe.wait_ge(stb_ready, g + (4 * l + 1))
                            pe.wait_ge(ye_act, g * 4 + (YE0 + NE * l + 4))
                            pe.wait_ge(ye_dve, g * 4 + (YE0 + NE * l + 4))
                            i = 0
                            for q in range(s.ns):
                                for j in range(2):
                                    for h in range(2):
                                        pe.wait_ge(sc_evicted, g * spg + (EV0 + sc0 + i - 1))
                                        mm(SCB[i % 2][:], STB[:, q, 128 * j:128 * j + 128], YE[:, q, 512 * h:512 * h + 512],
                                           start=True, stop=True).then_inc(sc_ready, 1)
                                        i += 1


_INS = ["x", "c", "ctx", "c_ctx", "w_ada", "b_ada", "g_mix", "w_in", "conv_w", "na_rpb", "sw_sink", "w_branch", "w_out",
        "g_ffn", "w_router", "w_exp_gate", "w_exp_up", "w_exp_down", "g_final"]


def kernel(**inputs):
    import numpy as _np
    import concourse.bacc as _bacc
    from concourse import mybir as _mybir
    from concourse.bass_utils import run_bass_kernel_spmd as _run

    nc = _bacc.Bacc("TRN2", target_bir_lowering=False, num_devices=1, dynamic_dma_scratch_size=4096)
    arrays, aps = {}, {}
    for name in _INS:
        a = _np.ascontiguousarray(inputs[name])
        arrays[f"in_{name}"] = a
        aps[name] = nc.dram_tensor(f"in_{name}", a.shape, _mybir.dt.from_np(a.dtype), kind="ExternalInput").ap()
    consts = shape_constants()
    arrays["consts"] = consts
    aps["consts"] = nc.dram_tensor("consts", consts.shape, _mybir.dt.float32, kind="ExternalInput").ap()
    out = nc.dram_tensor("out_0", (1, SEQ, D), _mybir.dt.float32, kind="ExternalOutput").ap()
    hybrid_dit_kernel(nc, aps, out)
    r = _run(nc, [arrays], core_ids=[0])
    return r.results[0]["out_0"]
```

```python
from contextlib import ExitStack

import numpy as np

import concourse.bass as bass
from concourse import mybir

D = 1024
SEQ = 256
CTX = 256
TOK = SEQ + CTX
DEPTH = 2
GRID_W = 64
HD = 64
BW = 512
NE = 16
FF = 1024
CAP = 2 * SEQ // NE
KD = D // 128
KB = BW // 128
NTT = TOK // 128
RPB_R, RPB_C = 15, 31
RPB_REP = 65
NEG = -1e30
EPS = 1e-6
SLOT = 4096
NSLOT = 6
SLAB = 56280
NWIN = 8
STREAM = [2, 3]
NBLK = 3
COL = dict(ab=0, ac=512, ax=1024, nq=1536, nk=2048, nv=2560, sq=3072, sk=3584, sv=3712, gate=3840)
SH1, SC1, GT1, SH2, SC2, GT2V = range(6)


def shape_constants():
    p = np.arange(128)
    ident = np.eye(128, dtype=np.float32)
    t = np.arange(SEQ)
    inv = (np.float32(10000.0) ** (-np.arange(16, dtype=np.float32) / np.float32(16))).astype(np.float32)
    ang = np.concatenate([(t // GRID_W).astype(np.float32)[:, None] * inv,
                          (t % GRID_W).astype(np.float32)[:, None] * inv], axis=1)
    rope = np.stack([np.cos(ang).T[p % 32], np.sin(ang).T[p % 32]], axis=1).astype(np.float32)
    rot = np.zeros((128, 128), np.float32)
    for o in range(128):
        if o % 64 < 32:
            rot[o + 32, o] = -1.0
        else:
            rot[o - 32, o] = 1.0
    q = p[:, None, None] + 128 * np.arange(2)[None, :, None]
    swmask = np.where(np.abs(q - t[None, None, :]) <= 128, 0.0, NEG).astype(np.float32)
    c = p[:, None] % GRID_W
    kc = t[None, :] % GRID_W
    start = np.clip(c - 8, 0, GRID_W - 16)
    namask = np.where((kc >= start) & (kc < start + 16), 0.0, NEG).astype(np.float32)
    sel = np.zeros((128, 2, 128), np.float32)
    for s in range(2):
        sel[s::32, s, :] = 1.0
    slots = np.tile(np.arange(1, CAP + 1, dtype=np.float32), (128, 1))
    flat = [ident, rope.reshape(128, -1), rot, swmask.reshape(128, -1), namask, sel.reshape(128, -1), slots]
    return np.ascontiguousarray(np.concatenate(flat, axis=1))


CONST_W = [128, 512, 128, 512, 256, 256, CAP]


class Step:

    def __init__(self, ac_tile=None, act=None, arrive=None, arrived=None, at=None, b=None, bank=None, before=None, bias=None,
                 bias_before=None, blk=None, br=None, c_tile=None, chunk=None, code=None, col=None, d=None, d_tile=None,
                 dve=None, end=None, expert=None, first=None, gate=None, grp=None, gt_free=None, half=None, hh=None, hts=None,
                 i=None, info=None, k=None, kind=None, kk=None, l=None, layer=None, lg=None, lt=None, mods=None, n=None, normalised=None,
                 nk=None, ns=None, ntt=None, o_ready=None, o_ready_need=None, ord=None, out=None, out_tile=None, p=None,
                 parts=None, pt_before=None, qt=None, ready=None, recent=None, ref=None, rope=None, rot_tile=None, s=None,
                 set=None, sets=None, slot=None, split_end=None, src=None, sum=None, tile=None, tiles=None, u=None, unit=None,
                 units=None, used_tile=None, v=None, v_ready=None, which=None, width=None, x_updated=None, xnh=None):
        self.ac_tile = ac_tile
        self.act = act
        self.arrive = arrive
        self.arrived = arrived
        self.at = at
        self.b = b
        self.bank = bank
        self.before = before
        self.bias = bias
        self.bias_before = bias_before
        self.blk = blk
        self.br = br
        self.c_tile = c_tile
        self.chunk = chunk
        self.code = code
        self.col = col
        self.d = d
        self.d_tile = d_tile
        self.dve = dve
        self.end = end
        self.expert = expert
        self.first = first
        self.gate = gate
        self.grp = grp
        self.gt_free = gt_free
        self.half = half
        self.hh = hh
        self.hts = hts
        self.i = i
        self.info = info
        self.k = k
        self.kind = kind
        self.kk = kk
        self.l = l
        self.layer = layer
        self.lg = lg
        self.lt = lt
        self.mods = mods
        self.n = n
        self.normalised = normalised
        self.nk = nk
        self.ns = ns
        self.ntt = ntt
        self.o_ready = o_ready
        self.o_ready_need = o_ready_need
        self.ord = ord
        self.out = out
        self.out_tile = out_tile
        self.p = p
        self.parts = parts
        self.pt_before = pt_before
        self.qt = qt
        self.ready = ready
        self.recent = recent
        self.ref = ref
        self.rope = rope
        self.rot_tile = rot_tile
        self.s = s
        self.set = set
        self.sets = sets
        self.slot = slot
        self.split_end = split_end
        self.src = src
        self.sum = sum
        self.tile = tile
        self.tiles = tiles
        self.u = u
        self.unit = unit
        self.units = units
        self.used_tile = used_tile
        self.v = v
        self.v_ready = v_ready
        self.which = which
        self.width = width
        self.x_updated = x_updated
        self.xnh = xnh


class Plan:

    def __init__(self):
        self.steps = [[] for _ in range(DEPTH + 1)]
        self.layer = 0
        self.tiles = self.act = self.dve = 0
        self.recent = [None] * NBLK
        self.blocks = []
        self.chunks = []
        self.arrive = [0] * NWIN
        self.top = 0
        self.occupants = []
        self.units = self.sets = self.biases = 0
        self.mods = 0
        self.bias_unit = [None] * 4
        self.ropes = 0
        self.obs = 0
        self.sums = 0
        self.gt_free = None
        self.pt_before = [None, None]
        self.deferred = []
        self.scored = self.turned = None

    def add(self, kind, **kw):
        s = Step(kind=kind, layer=self.layer, **kw)
        self.steps[self.layer].append(s)
        return s

    def tile(self, act=False, dve=False):
        n = self.tiles
        self.tiles += 1
        t = Step(n=n, bank=n % NBLK, before=self.recent[n % NBLK], ready=n + 1, act=None, dve=None)
        if act:
            self.act += 1
            t.act = self.act
        if dve:
            self.dve += 1
            t.dve = self.dve
        self.recent[n % NBLK] = t
        return t

    def load(self, parts):
        size = sum(shape[0] * shape[1] for _, shape, _ in parts)
        if self.top + size > STREAM[self.layer] * SLOT:
            self.top = 0
        lo, hi = self.top, self.top + size
        self.top = hi
        i = len(self.chunks) % NWIN
        self.arrive[i] += 16 * len(parts)
        before = [c for a, b, c in self.occupants if a < hi and lo < b]
        if len(self.chunks) >= NWIN:
            before.append(self.chunks[-NWIN])
        self.occupants = [o for o in self.occupants if not (lo <= o[0] and o[1] <= hi)]
        c = Step(n=i, at=lo, arrived=self.arrive[i], before=before, parts=parts, split_end=None, used_tile=None)
        self.occupants.append((lo, hi, c))
        self.chunks.append(c)
        self.add("load", chunk=c)
        return c

    def block(self, chunk, at, width, col, kk, n, src, out, tile, **kw):
        b = Step(b=len(self.blocks), chunk=chunk, at=at, width=width, col=col, kk=kk, n=n, src=src, tile=tile, out=out, **kw)
        self.blocks.append(b)
        chunk.split_end = b.b + 1
        return b

    def flush(self):
        todo, self.deferred = self.deferred, []
        for f in todo:
            f()


def ksteps(P, b):
    return [("k", b, k) for k in range(b.kk)]


WAHEAD = 2
NWS = WAHEAD + 1


def make_plan():
    P = Plan()

    def finish_block(b):
        if not b.tile.dve:
            P.flush()
        P.add("done", blk=b)
        P.flush()
        if b.out in ("v", "out"):
            def turn_back():
                b.out_tile = P.tile(dve=True)
                P.add("finish", blk=b)
            P.deferred.append(turn_back)
        elif b.out in ("sk", "sq"):
            def rope():
                b.rot_tile = P.tile(dve=True)
                P.ropes += 1
                b.rope = P.ropes
                b.info.ready = ("qk_ready", P.ropes)
                P.add("finish", blk=b)
            P.deferred.append(rope)

    def emit(atom):
        kind = atom[0]
        if kind == "k":
            P.add("k", blk=atom[1], k=atom[2])
        elif kind == "done":
            finish_block(atom[1])
        elif kind == "call":
            atom[1]()
        else:
            raise ValueError(kind)

    def run(atoms):
        for a in atoms:
            emit(a)

    def ada(l, c):
        def go():
            halves = [P.load([(0, (4, 512), ("w_ada", l, 512 * c, 512, 4 * r, 4))]) for r in range(2)]
            v, half = c // 2, c % 2
            mm = P.tile(dve=True)
            for ch in halves:
                ch.used_tile = mm.ready
            s = P.add("ada", l=l, v=v, half=half, chunk=halves, tile=mm)

            def turn():
                if v == GT2V:
                    s.out = [P.tile(dve=True) for _ in range(2)]
                else:
                    s.out = [P.tile(dve=True)]
                    P.mods += 1
                P.add("ada2", l=l, v=v, half=half, out=s.out, tile=mm)
            P.deferred.append(turn)
        return go

    for l in range(DEPTH):
        P.layer = l
        last = l == DEPTH - 1
        NT = SEQ if last else TOK
        P.first_tile = P.tiles
        if l == 0:
            P.add("pre", tile=P.tile(act=True))
            for c in range(4):
                ada(0, c)()
                P.flush()
                if c == 1:
                    P.add("norm", which=0, ntt=4)
        else:
            P.add("norm", which=0, ntt=4)
        for k in range(KD):
            P.add("trmod", which=0, k=k, ntt=4, tile=P.tile(act=True), mods=P.mods, hts=8 * l + k)

        def col_chunk(name, l=l):
            return [P.load([(0, (8, 256), ("w_in", l, COL[name] + 256 * r, 256))]) for r in range(2)]
        ac_tiles = []
        for name in ("ac", "ax", "ab"):
            ch = col_chunk(name)
            for i in range(KB):
                t = P.tile(act=name == "ac", dve=name != "ac")
                b = P.block(ch[i // 2], 0, 256, 128 * (i % 2), 8, NT, "h", name, t, i=i)
                if name == "ac":
                    ac_tiles[i:] = [t]
                b.ac_tile = ac_tiles[i]
                if name == "ab":
                    P.obs += 1
                    b.o_ready = P.obs
                run(ksteps(P, b) + [("done", b)])
        o_conv = P.obs

        ch = col_chunk("nv")
        sv = None
        for i in range(KB + 1):
            if i == KB:
                ch = P.load([(0, (8, 128), ("w_in", l, COL["sv"], 128))])
            b = P.block(ch[i // 2] if i < KB else ch, 0, 256 if i < KB else 128, 128 * (i % 2) if i < KB else 0, 8, TOK, "h", "v", P.tile(act=True), i=i)
            run(ksteps(P, b) + [("done", b)])
            sv = b

        def qk(br, p, l=l, NT=NT):
            info = Step(br=br, p=p)
            atoms = []
            if br == "na":
                ch = P.load([(0, (8, 128), ("w_in", l, COL["nq"] + 128 * p, 128)),
                             (1024, (8, 128), ("w_in", l, COL["nk"] + 128 * p, 128))])
                for j, (name, n) in enumerate((("nq", NT), ("nk", TOK))):
                    t = None
                    b = P.block(ch, 1024 * j, 128, 0, 8, n, "h", name, None, p=p, info=info)
                    atoms += [("call", (lambda b=b: open_tile(b, dict(act=True, dve=True))))] + ksteps(P, b)
                    def fin(b=b):
                        finish_block(b)
                        info.ready = ("dve_evicted", b.tile.dve)
                    atoms.append(("call", fin))
            else:
                names = (("sk", TOK),) if p == 0 else ()
                names += (("sq", NT),)
                parts = []
                for j, (name, n) in enumerate(names):
                    c = COL["sk"] if name == "sk" else COL["sq"] + 128 * p
                    parts.append((1024 * j, (8, 128), ("w_in", l, c, 128)))
                ch = P.load(parts)
                for j, (name, n) in enumerate(names):
                    b = P.block(ch, 1024 * j, 128, 0, 8, n, "h", name, None, p=p, info=info)
                    atoms += [("call", (lambda b=b: open_tile(b, dict(act=True))))] + ksteps(P, b)
                    atoms.append(("done", b))
            return info, atoms

        def open_tile(b, kw):
            b.tile = P.tile(**kw)

        def dpair(i, d2, l=l, NT=NT):
            gch = P.load([(0, (8, 256), ("w_in", l, COL["gate"] + D * i + 256 * d2, 256))])
            rch = P.load([(0, (4, 256), ("w_branch", l * 3 + i, 256 * d2, 256))])
            atoms = []
            for j in range(2):
                d = 2 * d2 + j
                g = P.block(gch, 0, 256, 128 * j, 8, NT, "h", "gate", None, i=i, d=d)
                atoms += [("call", (lambda b=g: open_tile(b, dict(act=True))))] + ksteps(P, g)
                r = P.block(rch, 0, 256, 128 * j, 4, NT, "o%d" % i, "br", None, i=i, d=d, gate=g)
                def fin_g(b=g):
                    b.gt_free = P.gt_free
                    finish_block(b)
                atoms.append(("call", fin_g))
                atoms += [("call", (lambda b=r: open_tile(b, dict(dve=True))))] + ksteps(P, r)
                def fin_r(b=r):
                    if i == 0:
                        P.gt_free = ("dve_evicted", b.tile.dve)
                    else:
                        P.sums += 1
                        P.gt_free = ("mrg_ready", P.sums)
                    b.sum = P.sums
                    finish_block(b)
                atoms.append(("call", fin_r))
            return atoms

        def attention(br, p, info, fill):
            units = []
            for grp in range(1 if last else 2):
                st = Step(br=br, p=p, grp=grp, set=P.sets, first=P.units + len(units), v_ready=sv.out_tile.dve)
                P.sets += 1
                P.obs += 1
                st.o_ready = P.obs
                st.pt_before = P.pt_before[grp]
                P.pt_before[grp] = P.sets
                for hh in range(2):
                    for j in range(2):
                        units.append(Step(br=br, p=p, hh=hh, qt=2 * grp + j, u=P.units + len(units), info=info,
                                          nk=TOK if grp == 0 else CTX, set=st, end=hh == 1 and j == 1, bias=None, layer=l))
                st.end = P.units + len(units)
            P.units += len(units)
            for x in units:
                if br == "na" and x.qt < 2:
                    P.biases += 1
                    x.bias = P.biases
                    x.at = P.biases % (4 if last else 2)
                    x.bias_before = P.bias_unit[x.at]
                    P.bias_unit[x.at] = x.u + 1
                    P.add("bias", unit=x)
            nk_atoms = sum(a[0] == "k" for a in fill)
            per = -(-nk_atoms // len(units)) if nk_atoms else 0
            fill = list(fill)

            def piece(x):
                n = 0
                while fill and n < per:
                    a = fill.pop(0)
                    emit(a)
                    n += a[0] == "k"
                    if a[0] == "k" and n == (4 if last else 2) * per // 10:
                        P.add("normalise", unit=x)
                        x.normalised = True
                while fill and fill[0][0] != "k":
                    emit(fill.pop(0))

            for i, x in enumerate(units):
                P.add("score", unit=x)
                piece(x)
                turn()
                if not x.normalised:
                    P.add("normalise", unit=x)
                P.scored = x
            run(fill)

        def turn():
            if P.turned:
                P.add("pv", set=P.turned.set)
                P.turned = None
            if P.scored:
                P.add("turn", unit=P.scored)
                if P.scored.end:
                    P.turned = P.scored
                P.scored = None

        P.o_need = {0: o_conv}
        info, atoms = qk("na", 0)
        run(atoms)
        for p in range(KB):
            if p + 1 < KB:
                nxt, atoms = qk("na", p + 1)
            else:
                nxt, atoms = qk("sw", 0)
            sums = dpair(0, p)
            if p == KB - 1:
                a, b = len(atoms) // 2, KD + 2
                sums = atoms[:a] + sums[:b] + atoms[a:] + sums[b:]
                atoms = []
            attention("na", p, info, atoms + sums)
            info = nxt
        o_na = P.obs
        for p in range(KB):
            nxt, atoms = qk("sw", p + 1) if p + 1 < KB else (None, [])
            sums = dpair(1, p)
            if last:
                mid = len(sums) // 2
                now = ((4,), (5, 6), (7,), (8, 9))[p]
                sums = sums[:mid] + [("call", ada(l, now[0]))] + sums[mid:] + [("call", ada(l, c)) for c in now[1:]]
            attention("sw", p, info, atoms + sums)
            info = nxt
        o_sw = P.obs
        turn()
        turn()
        extra = [ada(l, c) for c in ((10, 11) if last else (4, 5, 10, 11, 6, 7, 8, 9))]
        if not last:
            extra += [ada(l + 1, c) for c in range(4)]
        for d2 in range(4):
            atoms = dpair(2, d2)
            mid = len(atoms) // 2
            run(atoms[:mid])
            now = extra and not (last and d2 == 0)
            if now:
                extra.pop(0)()
            run(atoms[mid:])
            if d2 == 0:
                P.add("gt2_bias", l=l, sets=P.sets)
            if now:
                extra.pop(0)()
        P.c_tile = P.tiles
        stage_c_end = P.tiles
        for b in [x for x in P.blocks if x.src[0] == "o" and x.o_ready_need is None]:
            b.o_ready_need = {"o0": o_conv, "o1": o_na, "o2": o_sw}[b.src]
        for half in range(2):
            ch = [P.load([(0, (8, 256), ("w_out", l, 512 * half + 256 * r, 256))]) for r in range(2)]
            for i in range(4):
                b = P.block(ch[i // 2], 0, 256, 128 * (i % 2), 8, NT, "m", "out", P.tile(act=True), d=4 * half + i, ord=8 * l + 4 * half + i)
                run(ksteps(P, b))
                b.mods = P.mods
                run([("done", b)])
                if b.d == 5:
                    P.add("presquare", ntt=NT // 128, x_updated=half_updated.out_tile.dve)
                if b.d == 3:
                    half_updated = b
                if extra and i % 2:
                    extra.pop(0)()
        P.flush()
        dense_end = P.tiles
        x_updated = b.out_tile.dve

        ns = 1 if last else 2
        P.add("norm", which=1, ntt=2 * ns, x_updated=x_updated)
        for k in range(KD):
            P.add("trmod", which=1, k=k, ntt=2 * ns, tile=P.tile(act=True), mods=P.mods, hts=None)
        P.add("route", ns=ns, xnh=sum(4 if q < DEPTH - 1 else 2 for q in range(l + 1)), lg=P.tile(act=True), lt=P.tile(dve=True), at=P.tile(dve=True), code=P.tile(dve=True))
        for s in range(ns):
            for k in range(KD):
                P.add("gather", ns=ns, s=s, k=k, tile=P.tile(act=k % 2 == 0, dve=k % 2 == 1))
        P.add("gates", ns=ns, tiles=[[P.tile(act=gp == 0, dve=gp == 1) for gp in range(2)] for s in range(ns)])
        before = [[c for a, b, c in P.occupants if a < SLOT * (j + 1) and SLOT * j < b and c.expert is None] for j in range(STREAM[l])]
        m = P.add("moe", ns=ns, before=before, tiles=P.tiles,
                  c_tile=stage_c_end, d_tile=dense_end, recent=list(P.recent), act=P.act, dve=P.dve)
        P.occupants = [(SLOT * j, SLOT * (j + 1), Step(expert=l, slot=j)) for j in range(NSLOT)]
        P.recent = [None] * NBLK
        P.top = 0
    P.layer = DEPTH
    P.add("final")

    P.blocks = [s.blk for l in range(DEPTH) for s in P.steps[l] if s.kind == "k" and s.k == 0]
    for i, b in enumerate(P.blocks):
        b.b = i
        b.chunk.split_end = i + 1

    for l in range(DEPTH):
        out, layer_blocks = [], [s.blk for s in P.steps[l] if s.kind == "k" and s.k == 0]
        ahead = {a.b: c for a, c in zip(layer_blocks, layer_blocks[WAHEAD:])}
        for s in P.steps[l]:
            if s.kind == "k" and s.k == 0 and s.blk.b in ahead:
                out.append(Step(kind="split", layer=l, blk=ahead[s.blk.b]))
            if s.kind == "trmod" and s.which == 0 and s.k == 0:
                out += [Step(kind="split", layer=l, blk=b) for b in layer_blocks[:WAHEAD]]
            out.append(s)
        P.steps[l] = out
    return P


def hybrid_dit_kernel(nc, A, out):
    f32 = mybir.dt.float32
    f32r = mybir.dt.float32r
    ALU = mybir.AluOpType
    ACT = mybir.ActivationFunctionType
    AX = mybir.AxisListType
    P = make_plan()
    ctx = ExitStack()
    with ctx:
        slab = ctx.enter_context(nc.sbuf_tensor("slab", [128, SLAB], f32))
        del slab
        base = nc.sbuf_base - SLAB * 4
        cursor = [base]

        def region(nbytes):
            at = cursor[0]
            cursor[0] += nbytes
            assert cursor[0] <= base + SLAB * 4, cursor[0] - base
            return at

        def sb(name, shape, at, dt=f32):
            return nc.alloc_sbuf_tensor_at(name, shape, dt, offset=at)

        R_X = region(16384)
        R_RING = region(NSLOT * 16384)
        R_HT = region(32768)
        R_WS = region(8192 * NWS)
        R_MRG = region(16384)
        R_PT = region(12288)
        R_P = region(4096)
        R_BIAS = region(2048)
        R_GT = region(2048)
        R_QT = region(2048)
        R_VSW = region(2048)

        X = sb("X", [128, NTT, D], R_X)
        ring = sb("ring", [128, NSLOT * SLOT], R_RING)
        R_O = R_RING + 2 * 16384
        R_Q = R_RING + 4 * 16384
        OH, OL = [], []
        for l, (n, o_at) in enumerate(((TOK, R_O), (SEQ, R_O + 16384))):
            OH.append([sb(f"OH{l}{i}", [128, KB, n], o_at + 32 * n * i, f32r) for i in range(2)])
            OL.append([sb(f"OL{l}{i}", [128, KB, n], o_at + 32 * n * i + 16 * n, f32r) for i in range(2)])
        V = sb("V", [128, NTT, BW], R_Q)
        VS = sb("VS", [128, NTT, 128], R_VSW)
        dup = [sb(f"dup{i}", [128, 2, 2, TOK], R_Q + 8192 + 8192 * i, f32r) for i in range(2)]
        stk = [sb(f"stk{i}", [128, 2, TOK], R_Q + 24576 + 4096 * i, f32r) for i in range(2)]
        AC = sb("AC", [128, KB, TOK], R_Q + 8192)
        U = sb("U", [128, KB, 2, SEQ + 2], R_Q + 16384)
        MH = [sb(f"MH{l}", [128, KD, n], at_, f32r) for l, (n, at_) in enumerate(((TOK, R_Q), (SEQ, R_Q + 16384)))]
        ML = [sb(f"ML{l}", [128, KD, n], at_, f32r) for l, (n, at_) in enumerate(((TOK, R_Q + 16384), (SEQ, R_Q + 24576)))]
        RPBT = [sb(f"RPBT{l}", [8 * RPB_R, RPB_REP, RPB_C], R_O + 16384 + 8192 * l) for l in range(DEPTH)]
        tiled = [nc.dram_tensor(f"rpb_tiled{l}", (8 * RPB_R, RPB_REP * RPB_C), f32, kind="Internal").ap() for l in range(DEPTH)]
        HH = sb("HH", [128, KD, TOK], R_HT, f32r)
        HL = sb("HL", [128, KD, TOK], R_HT + 16384, f32r)
        WH = [sb(f"WH{i}", [128, KD, 128], R_WS + 8192 * i, f32r) for i in range(NWS)]
        WL = [sb(f"WL{i}", [128, KD, 128], R_WS + 8192 * i + 4096, f32r) for i in range(NWS)]
        MRG = sb("MRG", [128, KD, TOK], R_MRG)
        PTL = sb("PTL", [128, 2, 4, SEQ], R_PT)
        PTC = sb("PTC", [128, 2, 2, SEQ], R_PT + 8192)
        PB = [sb(f"PB{i}", [128, TOK], R_P + 2048 * i) for i in range(2)]
        FT = [sb(f"FT{i}", [128, TOK], R_P + 2048 * i) for i in range(2)]
        YT = [sb(f"YT{i}", [128, TOK], R_P + 2048 * i) for i in range(2)]
        CT = sb("CT", [128, 2, SEQ], R_P)
        BIAS = [sb(f"BIAS{i}", [128, SEQ], (R_BIAS if i < 2 else R_PT + 8192) + 1024 * i) for i in range(4)]
        GT = sb("GT", [128, TOK], R_GT)
        QT = sb("QT", [128, TOK], R_QT)
        VT = [sb(f"VT{i}", [128, TOK], at_) for i, at_ in enumerate((R_GT, R_QT))]
        MB = sb("MB", [128, TOK], R_PT + 8192)
        XN = sb("XN", [128, NTT, D], R_MRG)
        H2 = sb("H2", [128, KD, TOK], R_HT)
        SQ = sb("SQ", [128, NTT, D], R_HT + 16384)
        XNH = sb("XNH", [128, NTT, D], R_PT + 8192, f32r)
        XNL = sb("XNL", [128, NTT, D], R_MRG, f32r)
        LG = sb("LG", [128, TOK], R_HT + 23552)
        WK = sb("WK", [32, SEQ], R_HT + 18432)
        MASK = sb("MASK", [32, SEQ], R_HT + 19456)
        CUM = sb("CUM", [32, SEQ], R_HT + 20480)
        CODE = sb("CODE", [32, SEQ], R_HT + 21504)
        LGT = sb("LGT", [128, NTT, NE], R_HT + 16384)
        CODT = sb("CODT", [128, 2, 2, NE], R_HT + 22528)
        XE = [sb(f"XE{n}", [128, KD, NE, n * CAP], R_HT) for n in (1, 2)]
        SELT = sb("SELT", [128, 2, 2, NE, CAP], R_WS, f32r)
        SELG = sb("SELG", [128, 2, 2, NE, CAP], R_WS + 16384)
        ST = sb("ST", [128, 4, 2, SEQ], R_WS + 8192)
        GT2 = sb("GT2", [128, 2, D], R_PT)
        TH = sb("TH", [128, 512], R_PT + 8192)
        HID = sb("HID", [128, 512], R_PT + 10240)
        XEB = [sb(f"XEB{i}", [128, KD, 64], R_P + 2048 * i) for i in range(2)]
        HIDT = sb("HIDT", [128, KD, 64], R_BIAS)
        STB = sb("STB", [128, 2, SEQ], R_GT)
        YE = sb("YE", [128, 2, D], R_MRG)
        GF = sb("GF", [128, D], R_RING)
        CONST = sb("CONST", [128, sum(CONST_W)], region(4 * sum(CONST_W)))
        at = [sum(CONST_W[:i]) for i in range(len(CONST_W) + 1)]
        IDENT = CONST[:, at[0]:at[1]]
        ROPE = CONST[:, at[1]:at[2]].rearrange("p (a t) -> p a t", a=2)
        ROT = CONST[:, at[2]:at[3]]
        SWM = CONST[:, at[3]:at[4]].rearrange("p (a t) -> p a t", a=2)
        NAM = CONST[:, at[4]:at[5]]
        SELB = CONST[:, at[5]:at[6]].rearrange("p (a t) -> p a t", a=2)
        SLOTS = CONST[:, at[6]:at[7]]
        NROW2 = 16 + DEPTH * 12
        COLS = sb("COLS", [128, 128 + NROW2], region(4 * (128 + NROW2)))
        ROWS = sb("ROWS", [128, 2, 128], R_P)
        RPB = sb("RPB", [8 * RPB_R, DEPTH, RPB_C], R_QT)
        CS = sb("CS", [128, KD, 32], region(1024))
        MOD = sb("MOD", [128, DEPTH, 6, KD, 2], region(4 * DEPTH * 96))
        WRP = sb("WRP", [128, (DEPTH * KD + 1) * NE], region(4 * (DEPTH * KD + 1) * NE))
        WR = WRP[:, 0:DEPTH * KD * NE].rearrange("p (l k e) -> p l k e", l=DEPTH, k=KD)
        SINK = sb("SINK", [128, DEPTH, 8], region(4 * DEPTH * 8))
        AFF = sb("AFF", [128, 2, 2, NE], region(256))
        SM = sb("SM", [128, 116], region(464))
        SS, VV, SD, RS, NW = (SM[:, 4 * i:4 * i + 4] for i in range(5))
        RMX, RSUM = SM[:, 20:24], SM[:, 24:28]
        M8 = SM[0:32, 28:36]
        MX = [SM[:, 36 + 2 * i:38 + 2 * i] for i in range(2)]
        NM = [SM[:, 40 + i:41 + i] for i in range(2)]
        ES = [SM[:, 44 + 3 * i:47 + 3 * i] for i in range(2)]
        RSM = [SM[:, 50 + i:51 + i] for i in range(2)]
        RED = SM[:, 52:60].rearrange("p (k s) -> p k s", k=4)
        TC = SM[:, 60:76]
        T2 = SM[:, 76:92]
        PRIME = SM[:, 92:112]
        SS2 = SM[:, 112:116]
        BANK = [ctx.enter_context(nc.psum_tensor(f"bank{i}", [128, 512], f32)) for i in range(8)]
        BLK, SB_, TB, PVB = BANK[0:3], BANK[3:5], BANK[5:7], BANK[7]
        GAB, UAB, HTB, YAB, SCB = BANK[0:2], BANK[2:4], BANK[4], BANK[5], BANK[6:8]

        def sem(name):
            return ctx.enter_context(nc.semaphore(name))

        const_in = sem("const_in")
        x_in = sem("x_in")
        ctx_in = sem("ctx_in")
        late_const_in = sem("late_const_in")
        out_written = sem("out_written")
        blk_ready = sem("blk_ready")
        act_evicted = sem("act_evicted")
        dve_evicted = sem("dve_evicted")
        split_hi = sem("split_hi")
        split_lo = sem("split_lo")
        cond_tanh = sem("cond_tanh")
        cs_ready = sem("cs_ready")
        mod_ready = sem("mod_ready")
        gt2_in = sem("gt2_in")
        sq_ready = sem("sq_ready")
        var_ready = sem("var_ready")
        std_ready = sem("std_ready")
        rs_ready = sem("rs_ready")
        xn_ready = sem("xn_ready")
        xn_act = sem("xn_act")
        xnh_ready = sem("xnh_ready")
        xnl_ready = sem("xnl_ready")
        xnl_pool = sem("xnl_pool")
        ht_ready = sem("ht_ready")
        qk_hi = sem("qk_hi")
        qk_ready = sem("qk_ready")
        bias_in = [sem(f"bias_in{i}") for i in range(2)]
        bias_ready = sem("bias_ready")
        s_ready = sem("s_ready")
        max_ready = sem("max_ready")
        exp_ready = sem("exp_ready")
        norm_ready = sem("norm_ready")
        turn_ready = sem("turn_ready")
        pt_ready = sem("pt_ready")
        pv_ready = sem("pv_ready")
        o_hi = sem("o_hi")
        o_ready = sem("o_ready")
        mrg_ready = sem("mrg_ready")
        ml_ready = sem("ml_ready")
        aff_exp = sem("aff_exp")
        rpb_in = sem("rpb_in")
        rpb_tiled = sem("rpb_tiled")
        rpb_saved = sem("rpb_saved")
        aff_ready = sem("aff_ready")
        wr_padded = sem("wr_padded")
        code_ready = sem("code_ready")
        sel_ready = sem("sel_ready")
        gate_sel = sem("gate_sel")
        xe_ready = sem("xe_ready")
        tanh_ready = sem("tanh_ready")
        silu_ready = sem("silu_ready")
        hid_ready = sem("hid_ready")
        hid_turned = sem("hid_turned")
        hidt_ready = sem("hidt_ready")
        ye_ready = sem("ye_ready")
        stb_ready = sem("stb_ready")
        sc_ready = sem("sc_ready")
        x_added = sem("x_added")
        gf_in = sem("gf_in")
        dve_chain = sem("dve_chain")
        act_chain = sem("act_chain")
        zeroed = sem("zeroed")
        sem_named = {"dve_evicted": dve_evicted, "qk_ready": qk_ready, "mrg_ready": mrg_ready}
        w_in = [sem(f"w_in{j}") for j in range(NWIN)]
        expert_in = [sem(f"expert_in{j}") for j in range(NSLOT)]
        chunk_used = [sem(f"chunk_used{j}") for j in range(NSLOT)]
        USED0 = [1, 1, 1, 2, 1, 1]
        HID0 = TURN0 = YE0 = SC0 = X0 = 1
        NS = [2] * (DEPTH - 1) + [1]
        SPG = [4 * n for n in NS]
        SCB0 = [4 * sum(SPG[:l]) for l in range(DEPTH + 1)]

        def released(t):
            return (dve_evicted, t.dve) if t.dve else (act_evicted, t.act)

        def source(ref):
            name, i, c0, n = ref[:4]
            a = A[name]
            if name == "w_branch":
                a = a.rearrange("l b k n -> (l b) k n")
            rows = slice(128 * ref[4], 128 * (ref[4] + ref[5])) if len(ref) > 4 else slice(None)
            return a[i, rows, c0:c0 + n].rearrange("(k p) n -> p k n", p=128)

        def place(at_, shape):
            return ring[:, at_:at_ + shape[0] * shape[1]].rearrange("p (k n) -> p k n", k=shape[0])

        def block_weights(b):
            return place(b.chunk.at + b.at, (b.kk, b.width))[:, :, b.col:b.col + 128]

        def wait_released(engine, chunks):
            for o in chunks:
                if o.expert is not None:
                    engine.wait_ge(chunk_used[o.slot], USED0[o.slot] + NE * (o.expert + 1))
                elif o.used_tile:
                    engine.wait_ge(blk_ready, o.used_tile)
                else:
                    engine.wait_ge(split_lo, o.split_end)

        def bcast_rows(row):
            return bass.AP(tensor=row.tensor, offset=row.offset, ap=[[0, 128]] + list(row.ap))

        NCONST = 7
        block = ctx.enter_context(nc.Block())

        @block.sync
        def _(sp):
            sp.dma_start(CONST[:], A["consts"]).then_inc(const_in, 16)
            r96 = A["b_ada"].rearrange("l (r p) -> (l r) p", p=128)
            sp.dma_start(ROWS[0:96, 0, :], r96).then_inc(const_in, 16)
            sp.dma_start(ROWS[96:112, 0, :], A["g_mix"].rearrange("l (r p) -> (l r) p", p=128)).then_inc(const_in, 16)
            sp.dma_start(ROWS[112:128, 0, :], A["g_ffn"].rearrange("l (r p) -> (l r) p", p=128)).then_inc(const_in, 16)
            sp.dma_start(ROWS[0:8, 1, :], A["c"].rearrange("o (r p) -> (o r) p", p=128)).then_inc(const_in, 16)
            sp.dma_start(ROWS[8:16, 1, :], A["c_ctx"].rearrange("(r p) -> r p", p=128)).then_inc(const_in, 16)
            sp.dma_start(ROWS[16:NROW2, 1, :], A["conv_w"].rearrange("l t (r p) -> (l t r) p", p=128)).then_inc(const_in, 16)
            for l in range(DEPTH + 1):
                for s in P.steps[l]:
                    if s.kind == "load":
                        c = s.chunk
                        wait_released(sp, c.before)
                        for at_, shape, ref in c.parts:
                            sp.dma_start(place(c.at + at_, shape), source(ref)).then_inc(w_in[c.n], 16)
                        if s.chunk is P.chunks[3]:
                            sp.dma_start(X[:, 0:2, :], A["x"].rearrange("o (t p) d -> p (o t) d", p=128)).then_inc(x_in, 16)
                            sp.dma_start(X[:, 2:4, :], A["ctx"].rearrange("o (t p) d -> p (o t) d", p=128)).then_inc(ctx_in, 16)
                        if s.chunk is P.chunks[7]:
                            for l_ in range(DEPTH):
                                sp.dma_start(WR[:, l_, :, :], A["w_router"][l_].rearrange("(k p) e -> p k e", p=128)).then_inc(late_const_in, 16)
                            sp.dma_start(SINK[:].rearrange("p l h -> p (l h)"),
                                         bcast_rows(A["sw_sink"].rearrange("l h -> (l h)"))).then_inc(late_const_in, 16)
                    elif s.kind == "gt2_bias":
                        sp.wait_ge(pv_ready, s.sets)
                        row = A["b_ada"][s.l, GT2V * D:(GT2V + 1) * D]
                        for q in range(2):
                            sp.dma_start(GT2[:, q, :], bcast_rows(row)).then_inc(gt2_in, 16)
                    elif s.kind == "moe":
                        mats = (A["w_exp_gate"][l], A["w_exp_up"][l], A["w_exp_down"][l])

                        def expert_chunk(e, j):
                            return mats[j // 2][e, 512 * (j % 2):512 * (j % 2 + 1), :].rearrange("a (k p) n -> p (a k) n", p=128)

                        for j in range(NSLOT):
                            if j < STREAM[l]:
                                wait_released(sp, s.before[j])
                            else:
                                sp.wait_ge(blk_ready, s.c_tile if j < (4 if l == 0 else 5) else s.d_tile)
                            sp.dma_start(place(SLOT * j, (4, D)), expert_chunk(slice(0, 1), j)).then_inc(expert_in[j], 16)
                        with sp.Fori(1, NE) as e:
                            for j in range(NSLOT):
                                sp.wait_ge(chunk_used[j], e + (USED0[j] + NE * l))
                                sp.dma_start(place(SLOT * j, (4, D)), expert_chunk(bass.ds(e, 1), j)).then_inc(expert_in[j], 16)
                    elif s.kind == "final":
                        sp.wait_ge(chunk_used[0], USED0[0] + NE * DEPTH)
                        sp.dma_start(GF[:], bcast_rows(A["g_final"])).then_inc(gf_in, 16)
                        sp.wait_ge(x_added, X0 + SCB0[DEPTH] + 2)
                        sp.dma_start(out.rearrange("o (t p) d -> p (o t) d", p=128), XN[:, 0:2, :]).then_inc(out_written, 16)
                        sp.wait_ge(out_written, 16)

        @block.gpsimd
        def _(pool):
            waited_layer = 0
            turned_to = []

            def mask(x):
                if x.bias == 1:
                    pool.wait_ge(const_in, 16 * NCONST)
                pool.wait_ge(bias_in[x.bias % 2], 32 * ((x.bias + 1) // 2 if x.bias % 2 else x.bias // 2))
                nc.gpsimd.tensor_tensor(BIAS[x.at][:], BIAS[x.at][:], NAM, ALU.add).then_inc(bias_ready, 1)

            for l in range(DEPTH):
                pool.dma_start(RPB[:, l, :], A["na_rpb"][l].rearrange("h r c -> (h r) c")).then_inc(rpb_in, 16)
            pool.wait_ge(rpb_in, 16 * DEPTH)
            for l in range(DEPTH):
                nc.gpsimd.tensor_copy(RPBT[l][:], RPB[:, l, :].unsqueeze(1).broadcast_to((8 * RPB_R, RPB_REP, RPB_C))).then_inc(rpb_tiled, 1)
                pool.wait_ge(rpb_tiled, l + 1)
                pool.wait_ge(ht_ready, 1)
                pool.dma_start(tiled[l], RPBT[l][:].rearrange("p a c -> p (a c)")).then_inc(rpb_saved, 16)
            pool.wait_ge(rpb_saved, 16 * DEPTH)
            for l in range(DEPTH):
                for s in P.steps[l]:
                    if s.kind == "bias":
                        x = s.unit
                        if x.bias_before:
                            pool.wait_ge(max_ready, x.bias_before)
                        if l > waited_layer:
                            waited_layer = l
                            pool.wait_ge(x_added, X0 + SCB0[l])
                        h = 2 * x.p + x.hh
                        for rr in range(2):
                            r = 2 * x.qt + rr
                            off = tiled[l].offset + (h * RPB_R + 7 - r) * RPB_REP * RPB_C + 15
                            toeplitz = bass.AP(tensor=tiled[l].tensor, offset=off,
                                               ap=[[RPB_C - 1, GRID_W], [RPB_REP * RPB_C, 4], [1, GRID_W]])
                            pool.dma_start(BIAS[x.at][64 * rr:64 * rr + 64, :].rearrange("p (r k) -> p r k", r=4),
                                           toeplitz).then_inc(bias_in[x.bias % 2], 16)
                        turned_to.append(x)
                        if l < DEPTH - 1:
                            mask(turned_to.pop(0))
                        elif len(turned_to) > 1:
                            mask(turned_to.pop(0))
                    elif s.kind == "score" and turned_to:
                        mask(turned_to.pop(0))
                    elif s.kind == "route":
                        pool.wait_ge(blk_ready, s.lg.ready - 1)
                        pool.wait_ge(xnh_ready, s.xnh)
                        for tt in range(s.ns, 2 * s.ns):
                            last = nc.gpsimd.tensor_tensor(XNL[:, tt, :], XN[:, tt, :], XNH[:, tt, :].bitcast(f32), ALU.subtract)
                        last.then_inc(xnl_pool, 1)
                    elif s.kind == "moe":
                        tw = CAP * s.ns
                        xe = XE[s.ns - 1]
                        pool.wait_ge(act_evicted, s.act)
                        pool.wait_ge(dve_evicted, s.dve)
                        with pool.Fori(0, 4) as g:
                            pool.wait_ge(sc_ready, g * SPG[l] + (SC0 + SCB0[l]))
                            for eo in range(4):
                                pool.wait_ge(chunk_used[3], g * 4 + (USED0[3] + NE * l + eo - 1))
                                nc.gpsimd.tensor_copy(XEB[eo % 2][:, :, 0:tw],
                                                      xe[:, :, bass.ds(g * 4 + eo, 1), :].rearrange("p k a t -> p k (a t)")).then_inc(xe_ready, 1)
                                if eo == 0:
                                    nc.gpsimd.tensor_copy(STB[:, 0:s.ns, :],
                                                          ST[:, bass.ds(g, 1), 0:s.ns, :].rearrange("p a s t -> p (a s) t")).then_inc(stb_ready, 1)

        @block.scalar
        def _(act):
            chain = [0]
            norms = [0]

            def link(ins):
                chain[0] += 1
                ins.then_inc(act_chain, 1)
                act.wait_ge(act_chain, chain[0])

            def norm(s):
                nc.scalar.activation(PRIME[:, 15 + norms[0]:16 + norms[0]], SLOTS[:, 0:1], ACT.Sqrt)
                if s.which == 1:
                    act.wait_ge(dve_evicted, s.x_updated)
                for tt in range(s.ntt):
                    if s.which != 1 and s.layer > 0:
                        act.wait_ge(x_added, X0 + SCB0[s.layer] - SPG[s.layer - 1] + 2 * (tt + 1))
                    elif s.which == 0 and tt % 2 == 0:
                        act.wait_ge((x_in, ctx_in)[tt // 2], 16)
                    c = 512 if s.which == 1 else 0
                    last = nc.scalar.activation(SQ[:, tt, c:D], X[:, tt, c:D], ACT.Square, accum_out=SS[:, tt:tt + 1])
                last.then_inc(sq_ready, 1)
                norms[0] += 1
                act.wait_ge(var_ready, norms[0])
                nc.scalar.activation(SD[:, 0:s.ntt], VV[:, 0:s.ntt], ACT.Sqrt).then_inc(std_ready, 1)
                if s.kind == "norm":
                    act.wait_ge(rs_ready, norms[0])
                    for c in range(2):
                        for tt in range(s.ntt // 2, s.ntt):
                            last = nc.scalar.activation(XN[:, tt, 512 * c:512 * c + 512], X[:, tt, 512 * c:512 * c + 512], ACT.Copy, scale=RS[:, tt:tt + 1])
                        last.then_inc(xn_act, 1)

            for l in range(DEPTH + 1):
                for s in P.steps[l]:
                    kind = s.kind
                    if kind == "pre":
                        act.wait_ge(blk_ready, s.tile.ready)
                        link(nc.scalar.copy(COLS[:], BLK[s.tile.bank][:, 0:128 + NROW2]))
                        nc.scalar.activation(TC, COLS[:, 128:144], ACT.Tanh, scale=0.5).then_inc(act_evicted, 1)
                    elif kind == "split":
                        b = s.blk
                        act.wait_ge(w_in[b.chunk.n], b.chunk.arrived)
                        if b.b >= NWS:
                            act.wait_ge(blk_ready, P.blocks[b.b - NWS].tile.ready)
                        w = block_weights(b)
                        nc.scalar.copy(WH[b.b % NWS][:, 0:b.kk, :], w).then_inc(split_hi, 1)
                    elif kind == "norm":
                        norm(s)
                    elif kind == "presquare":
                        act.wait_ge(dve_evicted, s.x_updated)
                        for tt in range(s.ntt):
                            nc.scalar.activation(SQ[:, tt, 0:512], X[:, tt, 0:512], ACT.Square, accum_out=SS2[:, tt:tt + 1])
                    elif kind == "trmod":
                        act.wait_ge(blk_ready, s.tile.ready)
                        if s.k == 0:
                            act.wait_ge(mod_ready, s.mods)
                        if s.which == 0 and s.hts > 1:
                            act.wait_ge(ht_ready, s.hts - 1)
                        sh, sc = (SH1, SC1) if s.which == 0 else (SH2, SC2)
                        dst = FT[s.k % 2][:] if s.which == 0 else H2[:, s.k, :]
                        for q in range(s.ntt // 2):
                            last = nc.scalar.activation(dst[:, SEQ * q:SEQ * q + SEQ], BLK[s.tile.bank][:, SEQ * q:SEQ * q + SEQ], ACT.Identity,
                                                        scale=MOD[:, l, sc, s.k, q:q + 1], bias=MOD[:, l, sh, s.k, q:q + 1])
                        last.then_inc(act_evicted, 1)
                    elif kind == "done":
                        b = s.blk
                        if b.out in ("ac", "v", "nq", "nk", "sk", "sq", "gate", "out"):
                            act.wait_ge(blk_ready, b.tile.ready)
                            t = BLK[b.tile.bank]
                        if b.out == "ac":
                            nc.scalar.copy(AC[:, b.i, 0:b.n], t[:, 0:b.n]).then_inc(act_evicted, 1)
                        elif b.out == "v":
                            if l == 0 and b.i == 1:
                                act.wait_ge(rpb_tiled, DEPTH)
                            nc.scalar.copy(VT[b.i % 2][:], t[:]).then_inc(act_evicted, 1)
                        elif b.out == "nq":
                            for hh in range(2):
                                for half in range(2):
                                    last = nc.scalar.activation(dup[b.p % 2][64 * half:64 * half + 64, 0, hh, 0:b.n],
                                                                t[64 * hh:64 * hh + 64, 0:b.n], ACT.Copy, scale=HD ** -0.5)
                            last.then_inc(act_evicted, 1)
                        elif b.out == "nk":
                            for hh in range(2):
                                last = nc.scalar.copy(stk[b.p % 2][64 * hh:64 * hh + 64, hh, 0:b.n], t[64 * hh:64 * hh + 64, 0:b.n])
                            last.then_inc(act_evicted, 1)
                        elif b.out in ("sk", "sq"):
                            if b.rope > 1:
                                act.wait_ge(qk_ready, b.rope - 1)
                            nc.scalar.activation(QT[:, 0:b.n], t[:, 0:b.n], ACT.Copy,
                                                 scale=HD ** -0.5 if b.out == "sq" else 1.0).then_inc(act_evicted, 1)
                        elif b.out == "gate":
                            if b.gt_free:
                                act.wait_ge(sem_named[b.gt_free[0]], b.gt_free[1])
                            nc.scalar.activation(GT[:, 0:b.n], t[:, 0:b.n], ACT.Tanh, scale=0.5).then_inc(act_evicted, 1)
                        elif b.out == "out":
                            act.wait_ge(mod_ready, b.mods)
                            for q in range(b.n // SEQ):
                                last = nc.scalar.activation(YT[b.d % 2][:, SEQ * q:SEQ * q + SEQ], t[:, SEQ * q:SEQ * q + SEQ], ACT.Copy,
                                                            scale=MOD[:, l, GT1, b.d, q:q + 1])
                            last.then_inc(act_evicted, 1)
                    elif kind == "finish" and s.blk.rope:
                        b = s.blk
                        act.wait_ge(dve_evicted, b.rot_tile.dve)
                        if b.out == "sq":
                            for hh in range(2):
                                last = nc.scalar.copy(stk[b.p % 2][64 * hh:64 * hh + 64, hh, 0:b.n], QT[64 * hh:64 * hh + 64, 0:b.n])
                        else:
                            for hh in range(2):
                                for half in range(2):
                                    last = nc.scalar.copy(dup[0][64 * half:64 * half + 64, 0, hh, 0:b.n], QT[64 * hh:64 * hh + 64, 0:b.n])
                        last.then_inc(qk_hi, 1)
                    elif kind == "score":
                        x = s.unit
                        u2 = x.u % 2
                        act.wait_ge(max_ready, x.u + 1)
                        sc, p_ = SB_[u2], PB[u2]
                        if x.qt < 2:
                            nc.scalar.activation(p_[:, 0:SEQ], p_[:, 0:SEQ], ACT.Exp, bias=NM[u2], accum_out=ES[u2][:, 0:1])
                            last = nc.scalar.activation(p_[:, SEQ:TOK], sc[:, SEQ:TOK], ACT.Exp, bias=NM[u2], accum_out=ES[u2][:, 1:2])
                        else:
                            last = nc.scalar.activation(p_[:, 0:CTX], sc[:, 0:CTX], ACT.Exp, bias=NM[u2], accum_out=ES[u2][:, 0:1])
                        if x.br == "sw":
                            last = nc.scalar.activation(ES[u2][:, 2:3], SINK[:, l, 2 * x.p + x.hh:2 * x.p + x.hh + 1], ACT.Exp, bias=NM[u2])
                        last.then_inc(exp_ready, 1)
                    elif kind == "turn":
                        x = s.unit
                        act.wait_ge(turn_ready, x.u + 1)
                        if x.set.pt_before:
                            act.wait_ge(pv_ready, x.set.pt_before)
                        buf, nk = (PTL, 4) if x.set.grp == 0 else (PTC, 2)
                        j = x.qt % 2
                        nc.scalar.copy(buf[:, x.hh, :, 128 * j:128 * j + 128],
                                       TB[x.u % 2][:, 0:128 * nk].rearrange("p (k q) -> p k q", k=nk)).then_inc(pt_ready, 1)
                    elif kind == "pv":
                        st = s.set
                        act.wait_ge(pv_ready, st.set + 1)
                        ob = 1 if st.br == "na" else 0
                        nc.scalar.copy(OH[l][ob][:, st.p, SEQ * st.grp:SEQ * st.grp + SEQ], PVB[:, 0:SEQ]).then_inc(o_hi, 1)
                    elif kind == "route":
                        act.wait_ge(blk_ready, s.lg.ready)
                        n = SEQ * s.ns
                        nc.scalar.copy(LG[:, 0:n], BLK[s.lg.bank][:, 0:n]).then_inc(act_evicted, 1)
                        act.wait_ge(dve_evicted, s.lt.dve)
                        nc.scalar.activation(AFF[:, :, 0:s.ns, :], AFF[:, :, 0:s.ns, :], ACT.Exp).then_inc(aff_exp, 1)
                    elif kind == "gather" and s.tile.act:
                        act.wait_ge(blk_ready, s.tile.ready)
                        nc.scalar.activation(XE[s.ns - 1][:, s.k, :, CAP * s.s:CAP * s.s + CAP],
                                             BLK[s.tile.bank][:].rearrange("p (e t) -> p e t", e=NE), ACT.Identity,
                                             scale=MOD[:, l, SC2, s.k, s.s:s.s + 1], bias=MOD[:, l, SH2, s.k, s.s:s.s + 1]).then_inc(act_evicted, 1)
                    elif kind == "gates":
                        for q in range(s.ns):
                            t = s.tiles[q][0]
                            act.wait_ge(blk_ready, t.ready)
                            nc.scalar.copy(ST[:, 0:2, q, :], BLK[t.bank][:].rearrange("p (g t) -> p g t", g=2)).then_inc(act_evicted, 1)
                    elif kind == "moe":
                        G = 2 if s.ns == 2 else 4
                        tw, nw = 128 // G, D // G
                        with act.Fori(0, 4) as g:
                            for eo in range(4):
                                e0 = NE * l + eo
                                act.wait_ge(chunk_used[1], g * 4 + (USED0[1] + e0 + 1))
                                act.wait_ge(hid_ready, g * 4 + (HID0 + e0))
                                nc.scalar.activation(TH[:, 0:nw], GAB[eo % 2][:, 0:nw], ACT.Tanh, scale=0.5).then_inc(tanh_ready, 1)
                                act.wait_ge(hid_turned, g * 4 + (TURN0 + e0 + 1))
                                nc.scalar.activation(HIDT[:, :, 0:tw].rearrange("p (h c) t -> p c h t", h=G),
                                                     HTB[:, 0:8 * tw].rearrange("p (c h t) -> p c h t", h=G, t=tw), ACT.Copy, scale=0.5).then_inc(hidt_ready, 1)
                    elif kind == "final":
                        s.ntt = 2
                        norm(s)

        @block.vector
        def _(dve):
            chain = [0]
            counts = dict(norm=0, xnh=0, gt2=0)

            def link(ins):
                chain[0] += 1
                ins.then_inc(dve_chain, 1)
                dve.wait_ge(dve_chain, chain[0])

            def norm(ntt, halves):
                counts["norm"] += 1
                n = counts["norm"]
                dve.wait_ge(sq_ready, n)
                if halves:
                    link(nc.vector.tensor_tensor(SS[:, 0:ntt], SS[:, 0:ntt], SS2[:, 0:ntt], ALU.add))
                nc.vector.tensor_scalar(VV[:, 0:ntt], SS[:, 0:ntt], 1.0 / D, EPS, ALU.mult, ALU.add).then_inc(var_ready, 1)
                dve.wait_ge(var_ready, n)
                dve.wait_ge(std_ready, n)
                link(nc.vector.reciprocal(RS[:, 0:ntt], SD[:, 0:ntt]))
                link(nc.vector.tensor_tensor(NW[:, 0:ntt], RS[:, 0:ntt], RS[:, 0:ntt], ALU.mult))
                link(nc.vector.tensor_tensor(NW[:, 0:ntt], NW[:, 0:ntt], VV[:, 0:ntt], ALU.mult))
                link(nc.vector.tensor_scalar(NW[:, 0:ntt], NW[:, 0:ntt], -0.5, 1.5, ALU.mult, ALU.add))
                nc.vector.tensor_tensor(RS[:, 0:ntt], RS[:, 0:ntt], NW[:, 0:ntt], ALU.mult).then_inc(rs_ready, 1)
                dve.wait_ge(rs_ready, n)

            nc.vector.memset(WRP[:, DEPTH * KD * NE:], 0.0).then_inc(wr_padded, 1)
            for i, (sem_, n) in enumerate([(chunk_used[j], USED0[j]) for j in range(NSLOT)]
                            + [(hid_ready, HID0), (hid_turned, TURN0), (ye_ready, YE0),
                               (sc_ready, SC0), (x_added, X0)]):
                nc.vector.memset(PRIME[:, i:i + 1], 0.0).then_inc(sem_, n)

            for l in range(DEPTH + 1):
                for s in P.steps[l]:
                    kind = s.kind
                    if kind == "pre":
                        link(nc.vector.memset(CS[:], 0.0))
                        dve.wait_ge(act_evicted, s.tile.act)
                        link(nc.vector.scalar_tensor_tensor(T2, TC, 1.0, COLS[:, 128:144], ALU.add, ALU.mult))
                        nc.vector.tensor_scalar(CS[:, :, 0:2].rearrange("p k s -> p s k"), T2.rearrange("p (s k) -> p s k", s=2),
                                                0.5, None, ALU.mult).then_inc(cs_ready, 1)
                    elif kind == "split":
                        b = s.blk
                        dve.wait_ge(split_hi, b.b + 1)
                        w = block_weights(b)
                        nc.vector.tensor_tensor(WL[b.b % NWS][:, 0:b.kk, :], w, WH[b.b % NWS][:, 0:b.kk, :].bitcast(f32),
                                                ALU.subtract).then_inc(split_lo, 1)
                    elif kind == "ada":
                        dve.wait_ge(blk_ready, s.tile.ready)
                        nc.vector.tensor_copy(MB[:], BLK[s.tile.bank][:]).then_inc(dve_evicted, 1)
                    elif kind == "ada2":
                        if s.v == GT2V:
                            for q in range(2):
                                if counts["gt2"] < 32 * (s.l + 1):
                                    counts["gt2"] = 32 * (s.l + 1)
                                    dve.wait_ge(gt2_in, counts["gt2"])
                                dve.wait_ge(blk_ready, s.out[q].ready)
                                g2 = GT2[:, q, 512 * s.half:512 * s.half + 512]
                                nc.vector.tensor_tensor(g2, BLK[s.out[q].bank][:], g2, ALU.add).then_inc(dve_evicted, 1)
                        else:
                            dve.wait_ge(blk_ready, s.out[0].ready)
                            turned = BLK[s.out[0].bank][:].rearrange("p (k j c) -> p k c j", k=4, j=4)[:, :, 0:2, :]
                            nc.vector.tensor_reduce(RED, turned, AX.X, ALU.add).then_inc(dve_evicted, 1)
                            dve.wait_ge(dve_evicted, s.out[0].dve)
                            m = MOD[:, s.l, s.v, 4 * s.half:4 * s.half + 4, :]
                            c0 = 48 * s.l + 8 * s.v + 4 * s.half
                            bias = COLS[:, c0:c0 + 4].unsqueeze(2).broadcast_to((128, 4, 2))
                            add = nc.vector.tensor_tensor(m, RED, bias, ALU.add)
                            if s.v in (SH1, SH2):
                                add.then_inc(mod_ready, 1)
                            elif s.v == GT1:
                                link(add)
                                nc.vector.tensor_scalar(m, m, 0.5, None, ALU.mult).then_inc(mod_ready, 1)
                            else:
                                link(add)
                                c0 = (96 if s.v == SC1 else 112) + 8 * s.l + 4 * s.half
                                g = COLS[:, c0:c0 + 4].unsqueeze(2).broadcast_to((128, 4, 2))
                                link(nc.vector.tensor_scalar(m, m, 1.0, None, ALU.add))
                                nc.vector.tensor_tensor(m, m, g, ALU.mult).then_inc(mod_ready, 1)
                    elif kind == "norm":
                        norm(s.ntt, s.which == 1)
                        for c in range(2):
                            for tt in range(s.ntt // 2):
                                last = nc.vector.tensor_scalar(XN[:, tt, 512 * c:512 * c + 512], X[:, tt, 512 * c:512 * c + 512], RS[:, tt:tt + 1], None, ALU.mult)
                            last.then_inc(xn_ready, 1)
                        if s.which == 1:
                            dve.wait_ge(xn_ready, 2 * counts["norm"])
                            dve.wait_ge(xn_act, 2 * counts["norm"])
                            for tt in range(s.ntt):
                                nc.vector.tensor_copy(XNH[:, tt, :], XN[:, tt, :]).then_inc(xnh_ready, 1)
                                counts["xnh"] += 1
                    elif kind == "trmod" and s.which == 0:
                        dve.wait_ge(act_evicted, s.tile.act)
                        link(nc.vector.tensor_copy(HH[:, s.k, :], FT[s.k % 2][:]))
                        nc.vector.tensor_tensor(HL[:, s.k, :], FT[s.k % 2][:], HH[:, s.k, :].bitcast(f32), ALU.subtract).then_inc(ht_ready, 1)
                    elif kind == "done":
                        b = s.blk
                        if b.out in ("ax", "ab", "nq", "nk", "br"):
                            dve.wait_ge(blk_ready, b.tile.ready)
                            t = BLK[b.tile.bank]
                        ns = b.n // SEQ
                        if b.out == "ax":
                            if b.i == 0:
                                link(nc.vector.memset(U[:].rearrange("p i s t -> p (i s) t")[:, :, 0:1], 0.0))
                                link(nc.vector.memset(U[:].rearrange("p i s t -> p (i s) t")[:, :, SEQ + 1:SEQ + 2], 0.0))
                            dve.wait_ge(act_evicted, b.ac_tile.act)
                            nc.vector.tensor_tensor(U[:, b.i, 0:ns, 1:SEQ + 1], t[:, 0:b.n].rearrange("p (s t) -> p s t", s=ns),
                                                    AC[:, b.i, 0:b.n].rearrange("p (s t) -> p s t", s=ns), ALU.mult).then_inc(dve_evicted, 1)
                        elif b.out == "ab":
                            if b.i == 0:
                                dve.wait_ge(dve_evicted, b.tile.dve - 1)
                            else:
                                dve.wait_ge(o_ready, b.o_ready - 1)
                            tap = [COLS[:, 144 + 12 * l + 4 * k + b.i:145 + 12 * l + 4 * k + b.i] for k in range(3)]
                            ct = CT[:, 0:ns, :]
                            link(nc.vector.tensor_scalar(ct, U[:, b.i, 0:ns, 0:SEQ], tap[0], None, ALU.mult))
                            link(nc.vector.scalar_tensor_tensor(ct, U[:, b.i, 0:ns, 1:SEQ + 1], tap[1], ct, ALU.mult, ALU.add))
                            link(nc.vector.scalar_tensor_tensor(ct, U[:, b.i, 0:ns, 2:SEQ + 2], tap[2], ct, ALU.mult, ALU.add))
                            nc.vector.tensor_tensor(ct, ct, t[:, 0:b.n].rearrange("p (s t) -> p s t", s=ns), ALU.mult).then_inc(dve_evicted, 1)
                            dve.wait_ge(dve_evicted, b.tile.dve)
                            oh = OH[l][0][:, b.i, 0:b.n].rearrange("p (s t) -> p s t", s=ns)
                            ol = OL[l][0][:, b.i, 0:b.n].rearrange("p (s t) -> p s t", s=ns)
                            link(nc.vector.tensor_copy(oh, ct))
                            nc.vector.tensor_tensor(ol, ct, oh.bitcast(f32), ALU.subtract).then_inc(o_ready, 1)
                        elif b.out == "nq":
                            dve.wait_ge(act_evicted, b.tile.act)
                            for hh in range(2):
                                own = slice(64 * hh, 64 * hh + 64)
                                for half in range(2):
                                    last = nc.vector.scalar_tensor_tensor(dup[b.p % 2][64 * half:64 * half + 64, 1, hh, 0:b.n], t[own, 0:b.n], HD ** -0.5,
                                                                          dup[b.p % 2][own, 0, hh, 0:b.n].bitcast(f32), ALU.mult, ALU.subtract)
                            last.then_inc(dve_evicted, 1)
                        elif b.out == "nk":
                            dve.wait_ge(act_evicted, b.tile.act)
                            for hh in range(2):
                                own, other = slice(64 * hh, 64 * hh + 64), slice(64 - 64 * hh, 128 - 64 * hh)
                                last = nc.vector.tensor_tensor(stk[b.p % 2][other, hh, 0:b.n], t[own, 0:b.n],
                                                               stk[b.p % 2][own, hh, 0:b.n].bitcast(f32), ALU.subtract)
                            last.then_inc(dve_evicted, 1)
                        elif b.out == "br":
                            dve.wait_ge(act_evicted, b.gate.tile.act)
                            g, m = GT[:, 0:b.n], MRG[:, b.d, 0:b.n]
                            if b.i == 0:
                                nc.vector.scalar_tensor_tensor(m, g, 1.0, t[:, 0:b.n], ALU.add, ALU.mult).then_inc(dve_evicted, 1)
                            else:
                                nc.vector.scalar_tensor_tensor(g, g, 1.0, t[:, 0:b.n], ALU.add, ALU.mult).then_inc(dve_evicted, 1)
                                dve.wait_ge(dve_evicted, b.tile.dve)
                                nc.vector.tensor_tensor(m, m, g, ALU.add).then_inc(mrg_ready, 1)
                                if b.i == 2:
                                    dve.wait_ge(mrg_ready, b.sum)
                                    link(nc.vector.tensor_copy(MH[l][:, b.d, 0:b.n], m))
                                    nc.vector.tensor_tensor(ML[l][:, b.d, 0:b.n], m, MH[l][:, b.d, 0:b.n].bitcast(f32), ALU.subtract).then_inc(ml_ready, 1)
                    elif kind == "finish":
                        b = s.blk
                        ns = b.n // SEQ
                        if b.out == "v":
                            dve.wait_ge(blk_ready, b.out_tile.ready)
                            dst = V[:, :, 128 * b.i:128 * b.i + 128] if b.i < KB else VS[:]
                            nc.vector.tensor_copy(dst, BLK[b.out_tile.bank][:].rearrange("p (t c) -> p t c", t=NTT)).then_inc(dve_evicted, 1)
                        elif b.out in ("sk", "sq"):
                            dve.wait_ge(blk_ready, b.rot_tile.ready)
                            r = BLK[b.rot_tile.bank]
                            nc.vector.tensor_tensor(r[:, SEQ:2 * SEQ], r[:, 0:SEQ], ROPE[:, 1, :], ALU.mult)
                            link(nc.vector.tensor_tensor(QT[:, 0:SEQ], QT[:, 0:SEQ], ROPE[:, 0, :], ALU.mult))
                            nc.vector.tensor_tensor(QT[:, 0:SEQ], QT[:, 0:SEQ], r[:, SEQ:2 * SEQ], ALU.add).then_inc(dve_evicted, 1)
                            dve.wait_ge(qk_hi, b.rope)
                            for hh in range(2):
                                own, other = slice(64 * hh, 64 * hh + 64), slice(64 - 64 * hh, 128 - 64 * hh)
                                if b.out == "sq":
                                    last = nc.vector.tensor_tensor(stk[b.p % 2][other, hh, 0:b.n], QT[own, 0:b.n],
                                                                   stk[b.p % 2][own, hh, 0:b.n].bitcast(f32), ALU.subtract)
                                else:
                                    for half in range(2):
                                        last = nc.vector.tensor_tensor(dup[0][64 * half:64 * half + 64, 1, hh, 0:b.n], QT[own, 0:b.n],
                                                                       dup[0][own, 0, hh, 0:b.n].bitcast(f32), ALU.subtract)
                            last.then_inc(qk_ready, 1)
                        elif b.out == "out":
                            dve.wait_ge(blk_ready, b.out_tile.ready)
                            xs = X[:, 0:2 * ns, 128 * b.d:128 * b.d + 128]
                            nc.vector.tensor_tensor(xs, xs, BLK[b.out_tile.bank][:, 0:b.n].rearrange("p (t c) -> p t c", t=2 * ns), ALU.add).then_inc(dve_evicted, 1)
                    elif kind == "score":
                        x = s.unit
                        u2 = x.u % 2
                        sc, p_ = SB_[u2], PB[u2]
                        dve.wait_ge(s_ready, x.u + 1)
                        sink = SINK[:, l, 2 * x.p + x.hh:2 * x.p + x.hh + 1]
                        if x.br == "sw" and l == 0 and x.p == 0:
                            dve.wait_ge(late_const_in, 16 * (DEPTH + 1))
                        if x.qt < 2:
                            if x.u >= 2:
                                dve.wait_ge(turn_ready, x.u - 1)
                            if x.bias:
                                dve.wait_ge(bias_ready, x.bias)
                            add = BIAS[x.at][:] if x.bias else SWM[:, x.qt, :]
                            nc.vector.tensor_tensor_reduce(p_[:, 0:SEQ], sc[:, 0:SEQ], add, 1.0, sink if x.br == "sw" else -3e38,
                                                           ALU.add, ALU.max, MX[u2][:, 0:1])
                            link(nc.vector.tensor_reduce(MX[u2][:, 1:2], sc[:, SEQ:TOK], AX.X, ALU.max))
                            nc.vector.tensor_reduce(NM[u2], MX[u2], AX.X, ALU.max, negate=True).then_inc(max_ready, 1)
                        elif x.br == "na":
                            if x.u >= 2:
                                dve.wait_ge(turn_ready, x.u - 1)
                            nc.vector.tensor_reduce(NM[u2], sc[:, 0:CTX], AX.X, ALU.max, negate=True).then_inc(max_ready, 1)
                        else:
                            if x.u >= 2:
                                dve.wait_ge(turn_ready, x.u - 1)
                            link(nc.vector.tensor_reduce(MX[u2][:, 0:1], sc[:, 0:CTX], AX.X, ALU.max))
                            nc.vector.tensor_scalar(NM[u2], MX[u2][:, 0:1], sink, -1.0, ALU.max, ALU.mult).then_inc(max_ready, 1)
                    elif kind == "normalise":
                        x = s.unit
                        u2 = x.u % 2
                        dve.wait_ge(exp_ready, x.u + 1)
                        es, n = ES[u2], x.nk
                        if x.qt < 2 and x.br == "na":
                            link(nc.vector.tensor_tensor(RSM[u2], es[:, 0:1], es[:, 1:2], ALU.add))
                        elif x.qt < 2:
                            link(nc.vector.tensor_reduce(RSM[u2], es[:, 0:3], AX.X, ALU.add))
                        elif x.br == "sw":
                            link(nc.vector.tensor_tensor(RSM[u2], es[:, 0:1], es[:, 2:3], ALU.add))
                        else:
                            link(nc.vector.tensor_copy(RSM[u2], es[:, 0:1]))
                        link(nc.vector.reciprocal(RSM[u2], RSM[u2]))
                        nc.vector.tensor_scalar(PB[u2][:, 0:n], PB[u2][:, 0:n], RSM[u2], None, ALU.mult).then_inc(norm_ready, 1)
                    elif kind == "pv":
                        st = s.set
                        ob = 1 if st.br == "na" else 0
                        dve.wait_ge(o_hi, st.set + 1)
                        cols = slice(SEQ * st.grp, SEQ * st.grp + SEQ)
                        nc.vector.tensor_tensor(OL[l][ob][:, st.p, cols], PVB[:, 0:SEQ], OH[l][ob][:, st.p, cols].bitcast(f32), ALU.subtract).then_inc(o_ready, 1)
                    elif kind == "route":
                        ns, ntt = s.ns, 2 * s.ns
                        dve.wait_ge(blk_ready, s.lg.ready - 1)
                        dve.wait_ge(xnh_ready, counts["xnh"])
                        for tt in range(ns):
                            last = nc.vector.tensor_tensor(XNL[:, tt, :], XN[:, tt, :], XNH[:, tt, :].bitcast(f32), ALU.subtract)
                        last.then_inc(xnl_ready, 1)
                        groups = BLK[s.lt.bank][:, 0:128 * ntt].rearrange("p (t j r) -> p t r j", t=ntt, j=4)
                        lt = LGT[:, 0:ntt, :]
                        dve.wait_ge(blk_ready, s.lt.ready)
                        link(nc.vector.tensor_reduce(lt, groups[:, :, 0:NE, :], AX.X, ALU.add))
                        link(nc.vector.tensor_reduce(RMX[:, 0:ntt], lt, AX.X, ALU.max, negate=True))
                        aff = AFF[:, :, 0:ns, :]
                        nc.vector.tensor_tensor(aff.rearrange("p j s e -> p s j e"), lt.rearrange("p (s j) e -> p s j e", j=2),
                                                RMX[:, 0:ntt].rearrange("p (s j) -> p s j", j=2).unsqueeze(3).broadcast_to((128, ns, 2, NE)),
                                                ALU.add).then_inc(dve_evicted, 1)
                        dve.wait_ge(aff_exp, l + 1)
                        rs = RSUM[:, 0:ntt].rearrange("p (j s) -> p j s", j=2)
                        link(nc.vector.tensor_reduce(rs, aff, AX.X, ALU.add))
                        link(nc.vector.reciprocal(RSUM[:, 0:ntt], RSUM[:, 0:ntt]))
                        nc.vector.tensor_tensor(aff, aff, rs.unsqueeze(3).broadcast_to((128, 2, ns, NE)), ALU.mult).then_inc(aff_ready, 1)
                        R = NE * ns
                        dve.wait_ge(blk_ready, s.at.ready)
                        nc.vector.tensor_copy(WK[0:R, :], BLK[s.at.bank][0:R, 0:SEQ]).then_inc(dve_evicted, 1)
                        dve.wait_ge(dve_evicted, s.at.dve)
                        for _ in range(CAP // 8):
                            link(nc.vector.max(M8[0:R, :], WK[0:R, :]))
                            link(nc.vector.match_replace(WK[0:R, :], M8[0:R, :], WK[0:R, :], -1.0))
                        link(nc.vector.tensor_scalar(MASK[0:R, :], WK[0:R, :], 0.0, None, ALU.is_lt))
                        link(nc.vector.tensor_tensor_scan(CUM[0:R, :], MASK[0:R, :], MASK[0:R, :], 0.0, ALU.add, ALU.bypass))
                        nc.vector.tensor_tensor(CODE[0:R, :], CUM[0:R, :], MASK[0:R, :], ALU.mult).then_inc(code_ready, 1)
                        dve.wait_ge(blk_ready, s.code.ready)
                        nc.vector.tensor_copy(CODT[:, :, 0:ns, :].rearrange("p j s e -> p j (s e)"),
                                              BLK[s.code.bank][:, 0:64].rearrange("p (j r) -> p j r", j=2)[:, :, 0:R]).then_inc(dve_evicted, 1)
                        dve.wait_ge(dve_evicted, s.code.dve)
                        for j in range(2):
                            for q in range(ns):
                                last = nc.vector.tensor_tensor(SELT[:, j, q, :, :], CODT[:, j, q, :].unsqueeze(2).broadcast_to((128, NE, CAP)),
                                                               SLOTS.unsqueeze(1).broadcast_to((128, NE, CAP)), ALU.is_equal)
                        last.then_inc(sel_ready, 1)
                        dve.wait_ge(sel_ready, l + 1)
                        for j in range(2):
                            for q in range(ns):
                                last = nc.vector.tensor_tensor(SELG[:, j, q, :, :], SELT[:, j, q, :, :].bitcast(f32),
                                                               AFF[:, j, q, :].unsqueeze(2).broadcast_to((128, NE, CAP)), ALU.mult)
                        last.then_inc(gate_sel, 1)
                    elif kind == "gather" and s.tile.dve:
                        dve.wait_ge(blk_ready, s.tile.ready)
                        nc.vector.tensor_scalar(XE[s.ns - 1][:, s.k, :, CAP * s.s:CAP * s.s + CAP],
                                                BLK[s.tile.bank][:].rearrange("p (e t) -> p e t", e=NE),
                                                MOD[:, l, SC2, s.k, s.s:s.s + 1], MOD[:, l, SH2, s.k, s.s:s.s + 1],
                                                ALU.mult, ALU.add).then_inc(dve_evicted, 1)
                    elif kind == "gates":
                        for q in range(s.ns):
                            t = s.tiles[q][1]
                            dve.wait_ge(blk_ready, t.ready)
                            nc.vector.tensor_copy(ST[:, 2:4, q, :], BLK[t.bank][:].rearrange("p (g t) -> p g t", g=2)).then_inc(dve_evicted, 1)
                    elif kind == "moe":
                        G = 2 if s.ns == 2 else 4
                        tw, nw = 128 // G, D // G
                        spg, sc0 = SPG[l], SCB0[l]
                        with dve.Fori(0, 4) as g:
                            dve.wait_ge(x_added, g * spg + (X0 + sc0))
                            for eo in range(4):
                                e0 = NE * l + eo
                                dve.wait_ge(tanh_ready, g * 4 + (e0 + 1))
                                nc.vector.scalar_tensor_tensor(TH[:, 0:nw], TH[:, 0:nw], 1.0, GAB[eo % 2][:, 0:nw], ALU.add, ALU.mult).then_inc(silu_ready, 1)
                                dve.wait_ge(silu_ready, g * 4 + (e0 + 1))
                                dve.wait_ge(chunk_used[3], g * 4 + (USED0[3] + e0 + 1))
                                dve.wait_ge(hid_turned, g * 4 + (TURN0 + e0))
                                nc.vector.tensor_tensor(HID[:, 0:nw], TH[:, 0:nw], UAB[eo % 2][:, 0:nw], ALU.mult).then_inc(hid_ready, 1)
                                dve.wait_ge(chunk_used[5], g * 4 + (USED0[5] + e0 + 1))
                                for c in range(G):
                                    for q in range(s.ns):
                                        rows = slice(tw * c + 32 * q, tw * c + 32 * q + 32)
                                        last = nc.vector.tensor_tensor(YE[32 * eo:32 * eo + 32, q, nw * c:nw * c + nw], YAB[rows, 0:nw],
                                                                       GT2[32 * eo:32 * eo + 32, q, nw * c:nw * c + nw], ALU.mult)
                                last.then_inc(ye_ready, 1)
                            i = 0
                            for q in range(s.ns):
                                for j in range(2):
                                    for h in range(2):
                                        dve.wait_ge(sc_ready, g * spg + (SC0 + sc0 + i + 1))
                                        xs = X[:, 2 * q + j, 512 * h:512 * h + 512]
                                        nc.vector.tensor_tensor(xs, xs, SCB[i % 2][:], ALU.add).then_inc(x_added, 1)
                                        i += 1
                    elif kind == "final":
                        norm(2, False)
                        dve.wait_ge(gf_in, 16)
                        for tt in range(2):
                            nc.vector.scalar_tensor_tensor(XN[:, tt, :], X[:, tt, :], RS[:, tt:tt + 1], GF[:], ALU.mult, ALU.mult).then_inc(x_added, 1)

        @block.tensor
        def _(pe):
            mm = nc.tensor.matmul

            def open_tile(t):
                if t.before is not None:
                    sem_, v = released(t.before)
                    pe.wait_ge(sem_, v)
                return BLK[t.bank]

            xn = 0
            for l in range(DEPTH):
                first_block = True
                for s in P.steps[l]:
                    kind = s.kind
                    if kind == "pre":
                        pe.wait_ge(const_in, 16 * NCONST)
                        t = open_tile(s.tile)
                        nc.tensor.transpose(t[:, 0:128], ROWS[:, 0, :], IDENT)
                        nc.tensor.transpose(t[:, 128:128 + NROW2], ROWS[0:NROW2, 1, :], IDENT[0:NROW2, 0:NROW2]).then_inc(blk_ready, 1)
                        pe.wait_ge(cs_ready, 1)
                    elif kind == "ada":
                        t = open_tile(s.tile)
                        for ch in s.chunk:
                            pe.wait_ge(w_in[ch.n], ch.arrived)
                        w = [place(ch.at, (4, 512)) for ch in s.chunk]
                        for kk in range(2):
                            for j in range(4):
                                last = mm(t[32 * j:32 * j + 32, :], CS[:, 2 * j + kk, :], w[j // 2][:, 2 * (j % 2) + kk, :], start=kk == 0, stop=kk == 1,
                                          tile_position=(0, 32 * j))
                        last.then_inc(blk_ready, 1)
                    elif kind == "ada2":
                        pe.wait_ge(dve_evicted, s.tile.dve)
                        if s.v == GT2V:
                            for q in range(2):
                                t = open_tile(s.out[q])
                                mm(t[:], SELB[:, q, :], MB[:], start=True, stop=True).then_inc(blk_ready, 1)
                        else:
                            t = open_tile(s.out[0])
                            for k in range(4):
                                last = nc.tensor.transpose(t[:, 128 * k:128 * k + 128], MB[:, 128 * k:128 * k + 128], IDENT)
                            last.then_inc(blk_ready, 1)
                    elif kind == "norm":
                        xn += 2
                    elif kind == "trmod":
                        if s.k in (0, KD // 2):
                            for sem_ in (xn_ready, xn_act):
                                pe.wait_ge(sem_, xn - (s.k == 0))
                        t = open_tile(s.tile)
                        for tt in range(s.ntt):
                            last = nc.tensor.transpose(t[:, 128 * tt:128 * tt + 128], XN[:, tt, 128 * s.k:128 * s.k + 128], IDENT)
                        last.then_inc(blk_ready, 1)
                    elif kind == "k":
                        b, k = s.blk, s.k
                        if k == 0:
                            open_tile(b.tile)
                            pe.wait_ge(split_lo, b.b + 1)
                            if b.src[0] == "o":
                                pe.wait_ge(o_ready, b.o_ready_need)
                        if b.src == "m" and b.d == 0:
                            pe.wait_ge(ml_ready, KD * l + k + 1)
                        if first_block and b.src == "h":
                            pe.wait_ge(ht_ready, KD * l + k + 1)
                            first_block = k < KD - 1
                        hi, lo = {"h": (HH, HL), "m": (MH[l], ML[l]), "o0": (OH[l][0], OL[l][0]), "o1": (OH[l][1], OL[l][1]),
                                  "o2": (OH[l][0], OL[l][0])}[b.src]
                        t, wh, wl = BLK[b.tile.bank][:, 0:b.n], WH[b.b % NWS][:, k, :], WL[b.b % NWS][:, k, :]
                        mm(t, wh, hi[:, k, 0:b.n], start=k == 0, stop=False)
                        mm(t, wh, lo[:, k, 0:b.n], start=False, stop=False)
                        last = mm(t, wl, hi[:, k, 0:b.n], start=False, stop=k == b.kk - 1)
                        if k == b.kk - 1:
                            last.then_inc(blk_ready, 1)
                    elif kind == "finish":
                        b = s.blk
                        if b.out == "v" or b.out == "out":
                            pe.wait_ge(act_evicted, b.tile.act)
                            t, src = open_tile(b.out_tile), VT[b.i % 2] if b.out == "v" else YT[b.d % 2]
                            for tt in range(b.n // 128):
                                last = nc.tensor.transpose(t[:, 128 * tt:128 * tt + 128], src[:, 128 * tt:128 * tt + 128], IDENT)
                            last.then_inc(blk_ready, 1)
                        elif b.out in ("sk", "sq"):
                            pe.wait_ge(act_evicted, b.tile.act)
                            t = open_tile(b.rot_tile)
                            mm(t[:, 0:SEQ], ROT, QT[:, 0:SEQ], start=True, stop=True).then_inc(blk_ready, 1)
                    elif kind == "score":
                        x = s.unit
                        pe.wait_ge(sem_named[x.info.ready[0]], x.info.ready[1])
                        if x.u >= 2:
                            pe.wait_ge(exp_ready, x.u - 1)
                        q0, k0 = 128 * x.qt, TOK - x.nk
                        for part in range(2):
                            if x.br == "na":
                                q, k = dup[x.p % 2][:, part, x.hh, q0:q0 + 128], stk[x.p % 2][:, x.hh, k0:TOK]
                            else:
                                q, k = stk[x.p % 2][:, x.hh, q0:q0 + 128], dup[0][:, part, x.p // 2, k0:TOK]
                            last = mm(SB_[x.u % 2][:, 0:x.nk], q, k, start=part == 0, stop=part == 1)
                        last.then_inc(s_ready, 1)
                    elif kind == "turn":
                        x = s.unit
                        pe.wait_ge(norm_ready, x.u + 1)
                        if x.u >= 2:
                            pe.wait_ge(pt_ready, x.u - 1)
                        for c in range(x.nk // 128):
                            last = nc.tensor.transpose(TB[x.u % 2][:, 128 * c:128 * c + 128], PB[x.u % 2][:, 128 * c:128 * c + 128], IDENT)
                        last.then_inc(turn_ready, 1)
                    elif kind == "pv":
                        st = s.set
                        pe.wait_ge(pt_ready, st.end)
                        pe.wait_ge(dve_evicted, st.v_ready)
                        pe.wait_ge(o_ready, st.o_ready - 1)
                        buf, n = (PTL, 4) if st.grp == 0 else (PTC, 2)
                        for c in range(n):
                            for hh in range(2):
                                kt = c + 4 - n
                                v = V[:, kt, 128 * st.p + 64 * hh:128 * st.p + 64 * hh + 64] if st.br == "na" else \
                                    VS[:, kt, 64 * (st.p // 2):64 * (st.p // 2) + 64]
                                last = mm(PVB[64 * hh:64 * hh + 64, 0:SEQ], v, buf[:, hh, c, :], start=c == 0, stop=c == n - 1,
                                          tile_position=(0, 64 * hh))
                        last.then_inc(pv_ready, 1)
                    elif kind == "route":
                        n, R = SEQ * s.ns, NE * s.ns
                        t = open_tile(s.lg)
                        pe.wait_ge(act_evicted, s.lg.act - 1)
                        if l == 0:
                            pe.wait_ge(wr_padded, 1)
                            pe.wait_ge(late_const_in, 16 * (DEPTH + 1))
                        for kk in range(2):
                            for j in range(4):
                                c0 = (l * KD + 2 * j + kk) * NE
                                last = mm(t[32 * j:32 * j + 32, 0:n], WRP[:, c0:c0 + 32], H2[:, 2 * j + kk, 0:n], start=kk == 0, stop=kk == 1,
                                          tile_position=(0, 32 * j))
                        last.then_inc(blk_ready, 1)
                        pe.wait_ge(act_evicted, s.lg.act)
                        t = open_tile(s.lt)
                        for tt in range(2 * s.ns):
                            last = nc.tensor.transpose(t[:, 128 * tt:128 * tt + 128], LG[:, 128 * tt:128 * tt + 128], IDENT)
                        last.then_inc(blk_ready, 1)
                        pe.wait_ge(aff_ready, l + 1)
                        t = open_tile(s.at)
                        for j in range(2):
                            last = nc.tensor.transpose(t[0:R, 128 * j:128 * j + 128], AFF[:, j, 0:s.ns, :].rearrange("p s e -> p (s e)"), IDENT)
                        last.then_inc(blk_ready, 1)
                        pe.wait_ge(code_ready, l + 1)
                        t = open_tile(s.code)
                        for j in range(2):
                            last = nc.tensor.transpose(t[:, 32 * j:32 * j + R], CODE[0:R, 128 * j:128 * j + 128], IDENT[0:R, 0:R])
                        last.then_inc(blk_ready, 1)
                        pe.wait_ge(sel_ready, l + 1)
                    elif kind == "gather":
                        t = open_tile(s.tile)
                        if s.s == 0 and s.k == 0:
                            pe.wait_ge(xnl_ready, l + 1)
                            pe.wait_ge(xnl_pool, l + 1)
                        for j in range(2):
                            for part in (XNH, XNL):
                                last = mm(t[:], part[:, 2 * s.s + j, 128 * s.k:128 * s.k + 128],
                                          SELT[:, j, s.s, :, :].rearrange("p e t -> p (e t)"), start=j == 0 and part is XNH,
                                          stop=j == 1 and part is XNL)
                        last.then_inc(blk_ready, 1)
                    elif kind == "gates":
                        pe.wait_ge(gate_sel, l + 1)
                        for q in range(s.ns):
                            for gp in range(2):
                                t = open_tile(s.tiles[q][gp])
                                for g2 in range(2):
                                    e4 = 4 * (2 * gp + g2)
                                    for j in range(2):
                                        last = nc.tensor.transpose(t[:, 256 * g2 + 128 * j:256 * g2 + 128 * j + 128],
                                                                   SELG[:, j, q, e4:e4 + 4, :].rearrange("p e t -> p (e t)"), IDENT)
                                last.then_inc(blk_ready, 1)
                    elif kind == "moe":
                        G = 2 if s.ns == 2 else 4
                        tw, nw = 128 // G, D // G
                        spg, sc0 = SPG[l], SCB0[l]
                        pe.wait_ge(act_evicted, s.act)
                        pe.wait_ge(dve_evicted, s.dve)
                        with pe.Fori(0, 4) as g:

                            def product(out_bank, stationary, j0, e0, ready=None):
                                for k in range(KD):
                                    j = j0 + k // 4
                                    if k % 4 == 0:
                                        pe.wait_ge(expert_in[j], g * 64 + 16 * (e0 + 1))
                                    w = place(SLOT * j, (4, D))[:, k % 4, :]
                                    for c in range(G):
                                        last = mm(out_bank[tw * c:tw * c + tw, 0:nw], stationary[:, k, 0:tw], w[:, nw * c:nw * c + nw],
                                                  start=k == 0, stop=k == KD - 1, tile_position=(0, tw * c))
                                    if k % 4 == 3:
                                        last.then_inc(chunk_used[j], 1)

                            for eo in range(4):
                                e0 = NE * l + eo
                                pe.wait_ge(xe_ready, g * 4 + (e0 + 1))
                                product(GAB[eo % 2], XEB[eo % 2], 0, e0)
                                product(UAB[eo % 2], XEB[eo % 2], 2, e0)
                                pe.wait_ge(hid_ready, g * 4 + (HID0 + e0 + 1))
                                for c in range(8 // G):
                                    last = nc.tensor.transpose(HTB[:, 128 * c:128 * c + 128], HID[:, 128 * c:128 * c + 128], IDENT)
                                last.then_inc(hid_turned, 1)
                                pe.wait_ge(hidt_ready, g * 4 + (e0 + 1))
                                pe.wait_ge(ye_ready, g * 4 + (YE0 + e0))
                                product(YAB, HIDT, 4, e0)
                            pe.wait_ge(stb_ready, g + (4 * l + 1))
                            pe.wait_ge(ye_ready, g * 4 + (YE0 + NE * l + 4))
                            i = 0
                            for q in range(s.ns):
                                for j in range(2):
                                    for h in range(2):
                                        if i == 0 and l == 0:
                                            pe.wait_ge(x_added, g * spg + (X0 + sc0))
                                        else:
                                            pe.wait_ge(x_added, g * spg + (X0 + sc0 + i - 1))
                                        mm(SCB[i % 2][:], STB[:, q, 128 * j:128 * j + 128], YE[:, q, 512 * h:512 * h + 512],
                                           start=True, stop=True).then_inc(sc_ready, 1)
                                        i += 1


_INS = ["x", "c", "ctx", "c_ctx", "w_ada", "b_ada", "g_mix", "w_in", "conv_w", "na_rpb", "sw_sink", "w_branch", "w_out",
        "g_ffn", "w_router", "w_exp_gate", "w_exp_up", "w_exp_down", "g_final"]


def kernel(**inputs):
    import numpy as _np
    import concourse.bacc as _bacc
    from concourse import mybir as _mybir
    from concourse.bass_utils import run_bass_kernel_spmd as _run

    nc = _bacc.Bacc("TRN2", target_bir_lowering=False, num_devices=1, dynamic_dma_scratch_size=4096)
    arrays, aps = {}, {}
    for name in _INS:
        a = _np.ascontiguousarray(inputs[name])
        arrays[f"in_{name}"] = a
        aps[name] = nc.dram_tensor(f"in_{name}", a.shape, _mybir.dt.from_np(a.dtype), kind="ExternalInput").ap()
    consts = shape_constants()
    arrays["consts"] = consts
    aps["consts"] = nc.dram_tensor("consts", consts.shape, _mybir.dt.float32, kind="ExternalInput").ap()
    out = nc.dram_tensor("out_0", (1, SEQ, D), _mybir.dt.float32, kind="ExternalOutput").ap()
    hybrid_dit_kernel(nc, aps, out)
    r = _run(nc, [arrays], core_ids=[0])
    return r.results[0]["out_0"]
```
